# Optimizing a Trainium2 kernel written in Bass

```python
import jax, jax.numpy as jnp
from jax import lax
import numpy as np

D_MODEL = 2048
BATCH = 1
SEQ = 256
DEPTH = 1

MLA_HEADS = 16
MLA_QK_DIM = 128
MLA_V_DIM = 128
MLA_Q_RANK = 512
MLA_KV_RANK = 256
IDX_HEADS = 16
IDX_DIM = 64
IDX_TOPK_MAX = 256
Q_BLOCK = 128
GLA_HEADS = 4
GLA_KEY_DIM = D_MODEL // 2
GLA_VAL_DIM = D_MODEL
GLA_GATE_RANK = 16
GLA_GATE_TAU = 16.0
GLA_CHUNK = 64
FFN_HIDDEN = -(-8 * D_MODEL // (3 * 256)) * 256
N_MIXERS = 2
DEEPNORM_ALPHA = (2 * DEPTH) ** 0.25
DEEPNORM_BETA = (8 * DEPTH) ** -0.25
NORM_EPS = 1e-5

kernel_name = "hybrid_dsa_gla_deepnorm"

def _rms_norm(x, g):
    xf = x.astype(jnp.float32)
    y = xf * lax.rsqrt(jnp.mean(xf * xf, axis=-1, keepdims=True) + NORM_EPS)
    return (y * g.astype(jnp.float32)).astype(x.dtype)

def _layer_norm(x, g, b):
    xf = x.astype(jnp.float32)
    mu = jnp.mean(xf, axis=-1, keepdims=True)
    var = jnp.mean(jnp.square(xf - mu), axis=-1, keepdims=True)
    y = (xf - mu) * lax.rsqrt(var + NORM_EPS)
    return (y * g.astype(jnp.float32) + b.astype(jnp.float32)).astype(x.dtype)

def _swiglu(x, w_gate, w_up, w_down):
    return (jax.nn.silu(x @ w_gate) * (x @ w_up)) @ w_down

def _dsa_mixer(x, w_in, q_norm, kv_norm, w_uq, w_qidx, w_uk, w_uv, w_out):
    B, S, _ = x.shape
    topk = min(IDX_TOPK_MAX, S // 4)
    n_blocks = S // Q_BLOCK
    proj = x @ w_in
    c_q, c_kv, k_idx, w_idx = jnp.split(
        proj, [MLA_Q_RANK, MLA_Q_RANK + MLA_KV_RANK, MLA_Q_RANK + MLA_KV_RANK + IDX_DIM], axis=-1)
    c_q = _rms_norm(c_q, q_norm)
    c_kv = _rms_norm(c_kv, kv_norm)
    key_pos = jnp.arange(S)
    w_scale = IDX_HEADS ** -0.5
    d_scale = IDX_DIM ** -0.5
    attn_scale = MLA_QK_DIM ** -0.5

    def block(i):
        start = i * Q_BLOCK
        q_pos = start + jnp.arange(Q_BLOCK)
        cq = lax.dynamic_slice_in_dim(c_q, start, Q_BLOCK, axis=1)
        wq = lax.dynamic_slice_in_dim(w_idx, start, Q_BLOCK, axis=1)
        q_i = (cq @ w_qidx).reshape(B, Q_BLOCK, IDX_HEADS, IDX_DIM)
        logits = jnp.einsum('bqhd,bsd->bqhs', q_i, k_idx).astype(jnp.float32) * d_scale
        score = jnp.einsum('bqh,bqhs->bqs', wq.astype(jnp.float32) * w_scale, jax.nn.relu(logits))
        causal = key_pos[None, :] <= q_pos[:, None]
        score = jnp.where(causal[None], score, -jnp.inf)
        _, sel = lax.top_k(score, topk)
        valid = sel <= q_pos[None, :, None]
        kv_sel = jax.vmap(lambda c, ix: c[ix])(c_kv, sel)
        q = (cq @ w_uq).reshape(B, Q_BLOCK, MLA_HEADS, MLA_QK_DIM)
        q_lat = jnp.einsum('bqhd,hdr->bqhr', q, w_uk)
        s = jnp.einsum('bqhr,bqkr->bqhk', q_lat, kv_sel).astype(jnp.float32) * attn_scale
        s = jnp.where(valid[:, :, None, :], s, -jnp.inf)
        p = jax.nn.softmax(s, axis=-1).astype(x.dtype)
        o_lat = jnp.einsum('bqhk,bqkr->bqhr', p, kv_sel)
        return jnp.einsum('bqhr,hrv->bqhv', o_lat, w_uv)

    o = lax.map(block, jnp.arange(n_blocks))
    o = o.transpose(1, 0, 2, 3, 4).reshape(B, S, MLA_HEADS * MLA_V_DIM)
    return o @ w_out

def _gla_mixer(x, w_in, w_gk_up, b_gk, head_norm, w_out):
    B, S, _ = x.shape
    H = GLA_HEADS
    dk = GLA_KEY_DIM // H
    dv = GLA_VAL_DIM // H
    C = GLA_CHUNK
    n = S // C
    proj = x @ w_in
    q, k, v, r, g_lr = jnp.split(
        proj, [GLA_KEY_DIM, 2 * GLA_KEY_DIM, 2 * GLA_KEY_DIM + GLA_VAL_DIM,
               2 * GLA_KEY_DIM + 2 * GLA_VAL_DIM], axis=-1)
    log_a = jax.nn.log_sigmoid((g_lr @ w_gk_up + b_gk).astype(jnp.float32)) / GLA_GATE_TAU

    def to_chunks(t, d):
        return t.astype(jnp.float32).reshape(B, n, C, H, d).transpose(1, 0, 3, 2, 4)

    qc = to_chunks(q, dk) * (dk ** -0.5)
    kc = to_chunks(k, dk)
    vc = to_chunks(v, dv)
    gc = to_chunks(log_a, dk)
    tri = jnp.tril(jnp.ones((C, C), dtype=bool))

    def step(state, inp):
        qi, ki, vi, gi = inp
        b = jnp.cumsum(gi, axis=2)
        b_last = b[:, :, -1:, :]
        q_e = qi * jnp.exp(b)
        k_e = ki * jnp.exp(-b)
        intra = jnp.where(tri, jnp.einsum('bhik,bhjk->bhij', q_e, k_e), 0.0)
        o = jnp.einsum('bhik,bhkv->bhiv', q_e, state) + jnp.einsum('bhij,bhjv->bhiv', intra, vi)
        k_dec = ki * jnp.exp(b_last - b)
        state = jnp.exp(b_last[:, :, 0, :])[..., None] * state + jnp.einsum('bhjk,bhjv->bhkv', k_dec, vi)
        return state, o

    state0 = jnp.zeros((B, H, dk, dv), jnp.float32)
    _, o = lax.scan(step, state0, (qc, kc, vc, gc))
    o = o.transpose(1, 0, 3, 2, 4).reshape(B, S, H, dv)
    o = _rms_norm(o, head_norm).reshape(B, S, GLA_VAL_DIM).astype(x.dtype)
    return (o * jax.nn.silu(r)) @ w_out

def setup_inputs(seed: int = 0) -> dict:
    key = jax.random.key(seed)
    ks = iter(jax.random.split(key, 64))

    def nrm(shape, scale):
        return jax.random.normal(next(ks), shape, jnp.float32) * scale

    def gain(n):
        return 1.0 + nrm((n,), 0.02)

    D, F = D_MODEL, FFN_HIDDEN
    beta = DEEPNORM_BETA
    inp = {"x": nrm((BATCH, SEQ, D), 1.0)}
    inp["l0_w_in"] = nrm((D, MLA_Q_RANK + MLA_KV_RANK + IDX_DIM + IDX_HEADS), D ** -0.5)
    inp["l0_q_norm"] = gain(MLA_Q_RANK)
    inp["l0_kv_norm"] = gain(MLA_KV_RANK)
    inp["l0_w_uq"] = nrm((MLA_Q_RANK, MLA_HEADS * MLA_QK_DIM), MLA_Q_RANK ** -0.5)
    inp["l0_w_qidx"] = nrm((MLA_Q_RANK, IDX_HEADS * IDX_DIM), MLA_Q_RANK ** -0.5)
    inp["l0_w_uk"] = nrm((MLA_HEADS, MLA_QK_DIM, MLA_KV_RANK), MLA_KV_RANK ** -0.5)
    inp["l0_w_uv"] = nrm((MLA_HEADS, MLA_KV_RANK, MLA_V_DIM), MLA_KV_RANK ** -0.5)
    inp["l0_w_out"] = nrm((MLA_HEADS * MLA_V_DIM, D), beta * (MLA_HEADS * MLA_V_DIM) ** -0.5)
    inp["l0_ln1_g"] = gain(D)
    inp["l0_ln1_b"] = nrm((D,), 0.02)
    inp["l0_ffn_gate"] = nrm((D, F), D ** -0.5)
    inp["l0_ffn_up"] = nrm((D, F), D ** -0.5)
    inp["l0_ffn_down"] = nrm((F, D), beta * F ** -0.5)
    inp["l0_ln2_g"] = gain(D)
    inp["l0_ln2_b"] = nrm((D,), 0.02)
    inp["l1_w_in"] = nrm((D, 2 * GLA_KEY_DIM + 2 * GLA_VAL_DIM + GLA_GATE_RANK), D ** -0.5)
    inp["l1_w_gk_up"] = nrm((GLA_GATE_RANK, GLA_KEY_DIM), GLA_GATE_RANK ** -0.5)
    inp["l1_b_gk"] = nrm((GLA_KEY_DIM,), 0.1)
    inp["l1_head_norm"] = gain(GLA_VAL_DIM // GLA_HEADS)
    inp["l1_w_out"] = nrm((GLA_VAL_DIM, D), beta * GLA_VAL_DIM ** -0.5)
    inp["l1_ln1_g"] = gain(D)
    inp["l1_ln1_b"] = nrm((D,), 0.02)
    inp["l1_ffn_gate"] = nrm((D, F), D ** -0.5)
    inp["l1_ffn_up"] = nrm((D, F), D ** -0.5)
    inp["l1_ffn_down"] = nrm((F, D), beta * F ** -0.5)
    inp["l1_ln2_g"] = gain(D)
    inp["l1_ln2_b"] = nrm((D,), 0.02)
    return inp

def reference(x,
              l0_w_in, l0_q_norm, l0_kv_norm, l0_w_uq, l0_w_qidx, l0_w_uk, l0_w_uv, l0_w_out,
              l0_ln1_g, l0_ln1_b, l0_ffn_gate, l0_ffn_up, l0_ffn_down, l0_ln2_g, l0_ln2_b,
              l1_w_in, l1_w_gk_up, l1_b_gk, l1_head_norm, l1_w_out,
              l1_ln1_g, l1_ln1_b, l1_ffn_gate, l1_ffn_up, l1_ffn_down, l1_ln2_g, l1_ln2_b):
    layers = (
        ((l0_w_in, l0_q_norm, l0_kv_norm, l0_w_uq, l0_w_qidx, l0_w_uk, l0_w_uv, l0_w_out),
         (l0_ln1_g, l0_ln1_b, l0_ffn_gate, l0_ffn_up, l0_ffn_down, l0_ln2_g, l0_ln2_b)),
        ((l1_w_in, l1_w_gk_up, l1_b_gk, l1_head_norm, l1_w_out),
         (l1_ln1_g, l1_ln1_b, l1_ffn_gate, l1_ffn_up, l1_ffn_down, l1_ln2_g, l1_ln2_b)),
    )
    for i in range(DEPTH):
        mix_p, (ln1_g, ln1_b, w_gate, w_up, w_down, ln2_g, ln2_b) = layers[i]
        if i % N_MIXERS == 0:
            m = _dsa_mixer(x, *mix_p)
        else:
            m = _gla_mixer(x, *mix_p)
        x = _layer_norm(DEEPNORM_ALPHA * x + m, ln1_g, ln1_b)
        x = _layer_norm(DEEPNORM_ALPHA * x + _swiglu(x, w_gate, w_up, w_down), ln2_g, ln2_b)
    return x


_drawn_inputs = setup_inputs


def setup_inputs(seed=0):
    import zlib

    import numpy as np

    out = dict(_drawn_inputs(seed))
    spreads = {}
    factors = {'l0_q_norm': 5.219,
     'l0_kv_norm': 8.0,
     'l0_ln1_g': 2.674,
     'l0_ln1_b': 2.734,
     'l0_ln2_g': 2.791,
     'l0_ln2_b': 2.75}
    for name, (base, spread) in spreads.items():
        noise = np.random.default_rng([zlib.crc32(name.encode()), seed]).standard_normal(out[name].shape)
        drawn = base * np.exp(spread * noise) if base else spread * noise
        out[name] = __import__('jax').numpy.asarray(drawn.astype(out[name].dtype))
    for name, factor in factors.items():
        out[name] = (out[name] * factor).astype(out[name].dtype)
    return out
```

```python
from contextlib import ExitStack

import numpy as np

import concourse.bass as bass
from concourse import mybir

F32 = mybir.dt.float32
F32R = mybir.dt.float32r
ACT = mybir.ActivationFunctionType
ALU = mybir.AluOpType
AX = mybir.AxisListType

P = 128
D = 2048
S = 256
TOK = S // P
KD = D // P
Q_RANK = 512
KV_RANK = 256
IDX_DIM = 64
IDX_HEADS = 16
HEADS = 16
HD = 128
TOPK = min(256, S // 4)
FFN = 5632
KF = FFN // P
ALPHA = 2.0 ** 0.25
EPS = 1e-5
ATTN_SCALE = HD ** -0.5
IDX_SCALE = (IDX_HEADS ** -0.5) * (IDX_DIM ** -0.5)
W_IN = Q_RANK + KV_RANK + IDX_DIM + IDX_HEADS
KQ = Q_RANK // P
KV = KV_RANK // P
GH = 4
GROUPS = HEADS // GH
KEYS = S + P
MASKED = 1e30
NOT_CAUSAL = -3.0e38
TAKEN = -3.4e38

RAW_ELEMS = 2048
HALF = RAW_ELEMS // 2
RING = 4
R_IN = 0
X_BLOCKS = (0, 2)
IN_BLOCKS = (1, 3, 4, 5, 6, 7, 8, 9)
R_QIDX = 10
R_GROUP = 12
R_OUT = R_GROUP + 2 * GROUPS
R_FFN = R_OUT + KD
R_DOWN = R_FFN + 2 * KF
DOWN_K = (6, 5) * 4
X_HALVES = 2 * len(X_BLOCKS)

M_QIDX = 0
M_GROUP = M_QIDX + IDX_HEADS * IDX_DIM // P
M_PER_GROUP = 2 * GH + TOK
M_OUT = M_GROUP + GROUPS * M_PER_GROUP
M_DOWN = M_OUT + KD


def ring_index(v):
    x_before = sum(1 for b in X_BLOCKS for h in (0, 1) if 2 * b + h < v)
    return v - x_before


def layer_kernel(nc, a):
    ctx = ExitStack()
    with ctx:
        def sb(name, shape, dt=F32):
            return ctx.enter_context(nc.sbuf_tensor(name, shape, dt))

        def sem(name):
            return ctx.enter_context(nc.semaphore(name))

        raw = sb("raw", [P, RING, RAW_ELEMS])
        w_hi = sb("w_hi", [P, RING, HALF], F32R)
        w_lo = sb("w_lo", [P, RING, HALF], F32R)
        base_a = nc.sbuf_base
        act_t = sb("act_t", [P, KD, 2, S], F32R)
        base_r = nc.sbuf_base
        hid_t = sb("hid_t", [P, KF, 2, S], F32R)
        xn = sb("xn", [P, TOK, D])
        ident = sb("ident", [P, P])
        low = sb("low", [P, 2, S])
        comb = sb("comb", [P, 2, S])
        sig = sb("sig", [P, S])
        hid = sb("hid", [P, S])
        stats = sb("stats", [P, TOK, KD * 6])
        small = sb("small", [P, 24])
        ln1_gb = sb("ln1_gb", [P, 2, KD])

        def at(base):
            offset = [base]

            def place(name, shape, dt=F32):
                t = nc.alloc_sbuf_tensor_at(name, shape, dt, offset=offset[0])
                offset[0] += int(np.prod(shape[1:])) * 4
                return t
            return place

        place = at(base_a)
        q_t = place("q_t", [P, 2, GH, S])
        k_t = place("k_t", [P, 2, GH, S])
        v_n = place("v_n", [P, 2, TOK, GH * HD])
        score = place("score", [P, KEYS])
        work = place("work", [P, KEYS])
        key_bias = place("key_bias", [P, KEYS])
        top8 = place("top8", [P, TOK, 8])
        place = at(base_r)
        o_t = place("o_t", [P, HEADS, 2, S], F32R)
        PROJ = Q_RANK + KV_RANK + 2 * IDX_DIM + IDX_HEADS
        proj = place("proj", [P, TOK, PROJ])
        cq_t = place("cq_t", [P, KQ, 2, S], F32R)
        ckv_t = place("ckv_t", [P, KV, 2, S], F32R)
        kidx_t = place("kidx_t", [P, S])
        qidx_t = place("qidx_t", [P, IDX_HEADS * IDX_DIM // P, S])
        relu = place("relu", [P, 2, KEYS])
        neg_s = place("neg_s", [P, 2, KEYS])
        prob = place("prob", [P, 2, KEYS])
        prob_t = place("prob_t", [P, 2, KEYS])
        sq = place("sq", [P, Q_RANK])
        rms_g = place("rms_g", [P, KQ + KV])
        place = at(base_a)
        ln_rows = place("ln_rows", [P, 4, D])

        ssq = small[:, 0:4]
        rms_v = small[:, 4:8]
        rstd4 = small[:, 8:12]
        mean_var = small[:, 12:16]
        ln_v = small[:, 16:18]
        ln_s = small[:, 18:20]
        ln_r = small[:, 20:22]
        ln_nmr = small[:, 22:24]
        row_min = sb("row_min", [P, 2, TOK])
        row_sum = sb("row_sum", [P, 2, TOK])
        row_inv = sb("row_inv", [P, 2, TOK])

        acc = ctx.enter_context(nc.psum_tensor("acc", [P, 4, 512], F32))
        tp = ctx.enter_context(nc.psum_tensor("tp", [P, 4, 512], F32))

        raw_full = [sem(f"raw_full{i}") for i in range(RING)]
        const_full = sem("const_full")
        rms_full = sem("rms_full")
        xn_full = sem("xn_full")
        rows_full = sem("rows_full")
        out_done = sem("out_done")
        hi_done = sem("hi_done")
        lo_done = sem("lo_done")
        pe_used = sem("pe_used")
        ident_done = sem("ident_done")
        in_full = sem("in_full")
        ssq_done = sem("ssq_done")
        rms_var = sem("rms_var")
        rms_sqrt = sem("rms_sqrt")
        rms_inv = sem("rms_inv")
        proj_done = sem("proj_done")
        proj_t = sem("proj_t")
        c_hi = sem("c_hi")
        c_lo = sem("c_lo")
        acc_full = sem("acc_full")
        low_done = sem("low_done")
        comb_done = sem("comb_done")
        logits_full = sem("logits_full")
        relu_done = sem("relu_done")
        score_step = sem("score_step")
        score_masked = sem("score_masked")
        top_step = sem("top_step")
        bias_raw = sem("bias_raw")
        bias_done = sem("bias_done")
        qk_full = sem("qk_full")
        neg_done = sem("neg_done")
        min_done = sem("min_done")
        exp_done = sem("exp_done")
        inv_done = sem("inv_done")
        prob_done = sem("prob_done")
        pt_full = sem("pt_full")
        pt_done = sem("pt_done")
        pv_full = sem("pv_full")
        o_hi = sem("o_hi")
        o_lo = sem("o_lo")
        m_tp = sem("m_tp")
        res_done = sem("res_done")
        stat_done = sem("stat_done")
        aggr_done = sem("aggr_done")
        var_done = sem("var_done")
        sqrt_done = sem("sqrt_done")
        rstd_done = sem("rstd_done")
        xhat_done = sem("xhat_done")
        xt_full = sem("xt_full")
        xt_hi = sem("xt_hi")
        xt_val = sem("xt_val")
        xt_lo = sem("xt_lo")
        ffn_full = sem("ffn_full")
        ffn_low = sem("ffn_low")
        ffn_comb = sem("ffn_comb")
        ffn_sig = sem("ffn_sig")
        ffn_hid = sem("ffn_hid")
        ffn_hi = sem("ffn_hi")
        ffn_lo = sem("ffn_lo")
        x1_step = sem("x1_step")
        nmr_done = sem("nmr_done")
        y_norm = sem("y_norm")
        y_gain = sem("y_gain")
        y_done = sem("y_done")

        block = ctx.enter_context(nc.Block())

        in_raw = {b: n for n, b in enumerate(IN_BLOCKS)}
        hid_flat = hid_t[:].rearrange("p k h s -> p (k h s)")

        def flat(name):
            return a[name].rearrange("n p e -> (n p) e")

        w_out_rows, w_gu_rows, w_down_rows = flat("w_out"), flat("w_gu"), flat("w_down")

        def used_out(tile, half):
            return (pe_used, KD + tile + 1) if half == 0 else (acc_full, M_OUT + tile + 1)

        def used_ffn(tile, j):
            return (pe_used, 2 * KD + 3 * tile + j + 1) if j < 3 else (ffn_full, tile + 1)

        def used_down(tile, j):
            return (pe_used, 2 * KD + 3 * KF + 7 * tile + j + 1) if j < 7 else (acc_full, M_DOWN + tile + 1)

        def used_static(v):
            if v < 2 * R_QIDX:
                return pe_used, sum(1 for b in IN_BLOCKS for h in (0, 1) if 2 * b + h <= v)
            if v < 2 * R_GROUP:
                return acc_full, 2 * (v - 2 * R_QIDX) + 2
            if v < 2 * R_OUT:
                g, j = divmod(v - 2 * R_GROUP, 4)
                return acc_full, M_GROUP + g * M_PER_GROUP + (2, 4, 8, 10)[j]
            return used_out(*divmod(v - 2 * R_OUT, 2))

        @block.sync
        def _(sp):
            def load(r, slot, dst_elems, src, first=False):
                if not first:
                    sp.wait_ge(lo_done, 2 * r - 6)
                sp.dma_start(raw[:, slot, 0:dst_elems], src).then_inc(raw_full[slot], 16)

            for r in range(R_QIDX):
                if r in X_BLOCKS:
                    load(r, r % RING, RAW_ELEMS, a["x_t"][X_BLOCKS.index(r)], first=r < RING)
                else:
                    load(r, r % RING, 2 * W_IN, a["w_in"][in_raw[r]], first=r < RING)
            for n in range(2):
                load(R_QIDX + n, (R_QIDX + n) % RING, RAW_ELEMS, a["w_qidx"][n])
            for g in range(GROUPS):
                r = R_GROUP + 2 * g
                load(r, r % RING, RAW_ELEMS, a["w_uq"][g])
                load(r + 1, (r + 1) % RING, RAW_ELEMS, a["w_ukv"][g])
                if g == 0:
                    sp.dma_start(xn[:], a["x"].rearrange("(t p) d -> p t d", p=P)).then_inc(xn_full, 16)
            with sp.Fori(0, KD // RING) as i:
                for j in range(RING):
                    load(R_OUT + i * RING + j, j, RAW_ELEMS, w_out_rows[bass.ds((i * RING + j) * P, P), :])
            with sp.Fori(0, KF // 2) as i:
                for j in range(RING):
                    load(R_FFN + i * RING + j, j, RAW_ELEMS, w_gu_rows[bass.ds((i * RING + j) * P, P), :])
            for n in range(RING):
                load(R_DOWN + n, n, 11 * P, a["w_down"][n])
            sp.wait_ge(ffn_full, KF)
            for n in range(4):
                row = a["ln_rows"][n:n + 1, :].broadcast_to([P, D])
                sp.dma_start(ln_rows[:, n, :], row).then_inc(rows_full, 16)
            with sp.Fori(1, KD) as i:
                for j in range(RING):
                    load(R_DOWN + i * RING + j, j, 11 * P, w_down_rows[bass.ds((i * RING + j) * P, P), :])
            for c in range(4):
                for t in range(TOK):
                    sp.wait_ge(y_done, 2 * c + t + 1)
                    sp.dma_start(a["out"][t * P:(t + 1) * P, c * 512:(c + 1) * 512],
                                 xn[:, t, c * 512:(c + 1) * 512]).then_inc(out_done, 16)
            sp.wait_ge(out_done, 16 * 8)

        @block.scalar
        def _(act):
            act.dma_start(ln1_gb[:], a["ln1_gb_t"]).then_inc(const_full, 16)

            def hi_static(v):
                r, half = divmod(v, 2)
                if half == 0:
                    act.wait_ge(raw_full[r % RING], 16 * (r // RING + 1))
                if r in X_BLOCKS:
                    k0 = 8 * X_BLOCKS.index(r) + 4 * half
                    src = raw[:, r % RING, half * HALF:(half + 1) * HALF].rearrange("p (k s) -> p k s", s=S)
                    act.activation(act_t[:, k0:k0 + 4, 0, :], src, ACT.Copy).then_inc(hi_done, 1)
                    return
                w = ring_index(v)
                if w >= RING:
                    prev = next(u for u in range(v) if ring_index(u) == w - RING and u // 2 not in X_BLOCKS)
                    act.wait_ge(*used_static(prev))
                n = W_IN if r < R_QIDX else HALF
                act.activation(w_hi[:, w % RING, 0:n], raw[:, r % RING, half * n:(half + 1) * n],
                               ACT.Copy).then_inc(hi_done, 1)

            def take_low(m):
                act.wait_ge(acc_full, m + 1)
                if m >= 2:
                    act.wait_ge(comb_done, m - 1)
                act.activation(low[:, m % 2, :], acc[:, m % 4, S:2 * S], ACT.Copy).then_inc(low_done, 1)

            for v in range(2 * R_QIDX):
                hi_static(v)
            hi_static(2 * R_QIDX)
            hi_static(2 * R_QIDX + 1)

            act.wait_ge(pe_used, KD)
            for t in range(TOK):
                act.activation(sq[:, 0:Q_RANK], acc[:, 2 * t, :], ACT.Square,
                               accum_out=ssq[:, 2 * t:2 * t + 1]).then_inc(ssq_done, 1)
                act.wait_ge(ssq_done, 2 * t + 1)
                act.activation(sq[:, 0:KV_RANK], acc[:, 2 * t + 1, 0:KV_RANK], ACT.Square,
                               accum_out=ssq[:, 2 * t + 1:2 * t + 2]).then_inc(ssq_done, 1)
                act.wait_ge(ssq_done, 2 * t + 2)
            act.wait_ge(rms_var, 2)
            act.activation(rms_v, rstd4, ACT.Sqrt).then_inc(rms_sqrt, 1)
            for t in range(TOK):
                c = Q_RANK + KV_RANK
                act.activation(proj[:, t, c:c + IDX_DIM], acc[:, 2 * t + 1, KV_RANK:KV_RANK + IDX_DIM],
                               ACT.Copy).then_inc(proj_done, 1)
                act.activation(proj[:, t, c + IDX_DIM:c + 2 * IDX_DIM + IDX_HEADS],
                               acc[:, 2 * t + 1, KV_RANK:KV_RANK + IDX_DIM + IDX_HEADS],
                               ACT.Copy).then_inc(proj_done, 1)
            act.wait_ge(rms_inv, 1)
            for t in range(TOK):
                act.activation(proj[:, t, Q_RANK:Q_RANK + KV_RANK], acc[:, 2 * t + 1, 0:KV_RANK], ACT.Copy,
                               scale=rstd4[:, 2 * t + 1:2 * t + 2]).then_inc(proj_done, 1)
            act.wait_ge(rms_full, 16)
            act.wait_ge(const_full, 16)
            for n in range(KQ + KV):
                act.wait_ge(proj_t, (n | 1) + 1)
                dst = cq_t[:, n, 0, :] if n < KQ else ckv_t[:, n - KQ, 0, :]
                act.activation(dst, tp[:, n // 2, (n % 2) * S:(n % 2 + 1) * S], ACT.Copy,
                               scale=rms_g[:, n:n + 1]).then_inc(c_hi, 1)
            act.wait_ge(proj_t, KQ + KV + 1)
            act.activation(kidx_t[:], tp[:, 3, 0:S], ACT.Copy).then_inc(c_hi, 1)
            hi_static(2 * R_QIDX + 2)
            hi_static(2 * R_QIDX + 3)
            for m in range(M_GROUP):
                take_low(m)
                if m % 2 == 1:
                    hi_static(2 * R_GROUP + m // 2)
            for h in range(IDX_HEADS):
                act.wait_ge(logits_full, h + 1)
                if h >= 2:
                    act.wait_ge(score_step, 2 * (h - 1))
                act.activation(relu[:, h % 2, :], tp[:, h % 4, 0:KEYS], ACT.Relu,
                               scale=IDX_SCALE).then_inc(relu_done, 1)

            def piece(s):
                g, j = divmod(s, 4)
                m0 = M_GROUP + g * M_PER_GROUP
                if j < 3:
                    for m in {0: (0, 1), 1: (2, 3), 2: (4, 5, 6, 7)}[j]:
                        take_low(m0 + m)
                else:
                    for t in range(TOK):
                        m = m0 + 8 + t
                        act.wait_ge(acc_full, m + 1)
                        act.activation(v_n[:, g % 2, t, 0:S], acc[:, m % 4, 0:S], ACT.Copy)\
                           .then_inc(low_done, 1)

            for s in range(4):
                piece(s)
                hi_static(2 * R_GROUP + 4 + s)
            for s in range(HEADS + 2):
                if s + 4 < HEADS:
                    piece(s + 4)
                    hi_static(2 * R_GROUP + 8 + s)
                if s < HEADS:
                    for t in range(TOK):
                        act.wait_ge(min_done, 2 * s + t + 1)
                        cols = slice(0, P) if t == 0 else slice(P, KEYS)
                        act.activation(prob[:, s % 2, cols], neg_s[:, s % 2, cols], ACT.Exp, scale=-1.0,
                                       bias=row_min[:, s % 2, t:t + 1],
                                       accum_out=row_sum[:, s % 2, t:t + 1]).then_inc(exp_done, 1)
                if 1 <= s <= HEADS:
                    act.wait_ge(pt_full, s)
                    if s >= 3:
                        act.wait_ge(pv_full, s - 2)
                    act.activation(prob_t[:, (s - 1) % 2, :], tp[:, 2, 0:KEYS], ACT.Copy).then_inc(pt_done, 1)
                if s >= 2:
                    act.wait_ge(pv_full, s - 1)
                    act.activation(o_t[:, s - 2, 0, :], tp[:, 3, (s % 2) * S:(s % 2 + 1) * S], ACT.Copy)\
                       .then_inc(o_hi, 1)

            def hi_loop(used, raw_count, half, slot, n=HALF, first=None):
                first = half * n if first is None else first
                if half == 0:
                    act.wait_ge(raw_full[slot], 16 * raw_count)
                act.wait_ge(*used)
                act.activation(w_hi[:, (2 * slot + half) % RING, 0:n], raw[:, slot, first:first + n],
                               ACT.Copy).then_inc(hi_done, 1)

            def take_low_loop(m, bank, c):
                act.wait_ge(acc_full, m + 1)
                act.wait_ge(comb_done, m - 1)
                act.activation(low[:, c, :], acc[:, bank, S:2 * S], ACT.Copy).then_inc(low_done, 1)

            def out_tile(c, i):
                tile = RING * i + c
                for half in (0, 1):
                    hi_loop(used_out(tile - 2, half), R_OUT // RING + 1 + i, half, c)
                take_low_loop(M_OUT + tile - 2, (c - 2) % 4, c % 2)

            out_tile(2, 0)
            out_tile(3, 0)
            with act.Fori(1, KD // RING) as i:
                for c in range(RING):
                    out_tile(c, i)
            for c in range(2):
                for half in (0, 1):
                    hi_loop(used_out(KD - 2 + c, half), R_FFN // RING + 1, half, c)
                take_low_loop(M_OUT + KD - 2 + c, 2 + c, c)

            act.wait_ge(var_done, 1)
            act.activation(ln_s, ln_v, ACT.Sqrt).then_inc(sqrt_done, 1)
            for k in range(KD):
                act.wait_ge(xt_full, (k | 1) + 1)
                act.activation(act_t[:, k, 0, :], tp[:, (k // 2) % 4, (k % 2) * S:(k % 2 + 1) * S],
                               ACT.Identity, scale=ln1_gb[:, 0, k:k + 1],
                               bias=ln1_gb[:, 1, k:k + 1]).then_inc(xt_hi, 1)

            def ffn_low_step(tile, c):
                act.wait_ge(ffn_full, tile + 1)
                act.activation(low[:], acc[:, 2 * c:2 * c + 2, S:2 * S], ACT.Copy).then_inc(ffn_low, 1)

            def ffn_silu_step(tile):
                act.wait_ge(ffn_comb, tile + 1)
                act.activation(sig[:], comb[:, 0, :], ACT.Silu).then_inc(ffn_sig, 1)

            def ffn_hi_step(tile):
                act.wait_ge(ffn_hid, tile + 1)
                act.activation(hid_flat[:, bass.ds(tile * 2 * S, S)], hid[:], ACT.Copy).then_inc(ffn_hi, 1)

            def ffn_tile(c, i, older=True):
                tile = 2 * i + c
                for j in range(4):
                    hi_loop(used_ffn(tile - 1, j), R_FFN // RING + 1 + i, j % 2, 2 * c + j // 2)
                    if j == 0 and older:
                        ffn_silu_step(tile - 2)
                    if j == 1 and older:
                        ffn_hi_step(tile - 2)
                ffn_low_step(tile - 1, 1 - c)

            ffn_tile(1, 0, older=False)
            with act.Fori(1, KF // 2) as i:
                ffn_tile(0, i)
                ffn_tile(1, i)

            def down_half(j, i):
                used = used_down(i, j - 4) if j >= 4 else \
                    used_ffn(KF - 1, j) if isinstance(i, int) and i == 0 else used_down(i - 1, j + 4)
                hi_loop(used, R_DOWN // RING + 1 + i, j % 2, j // 2,
                        n=DOWN_K[j] * P, first=(j % 2) * DOWN_K[0] * P)

            for j in range(8):
                down_half(j, 0)
                if j == 0:
                    ffn_silu_step(KF - 2)
                if j == 1:
                    ffn_hi_step(KF - 2)
                if j == 3:
                    ffn_low_step(KF - 1, 1)
                    ffn_silu_step(KF - 1)
                    ffn_hi_step(KF - 1)

            def down_tile(c, i):
                for j in range(8):
                    down_half(j, 2 * i + c)
                    if j == 3:
                        take_low_loop(M_DOWN + 2 * i + c - 1, 1 - c, 1 - c)

            down_tile(1, 0)
            with act.Fori(1, KD // 2) as i:
                down_tile(0, i)
                down_tile(1, i)
            take_low_loop(M_DOWN + KD - 1, 1, 1)

            act.wait_ge(var_done, 2)
            act.activation(ln_s, ln_v, ACT.Sqrt).then_inc(sqrt_done, 1)
            act.wait_ge(nmr_done, 1)
            for c in range(4):
                for t in range(TOK):
                    piece_ = xn[:, t, c * 512:(c + 1) * 512]
                    act.activation(piece_, piece_, ACT.Identity, scale=ln_r[:, t:t + 1],
                                   bias=ln_nmr[:, t:t + 1]).then_inc(y_norm, 1)

        @block.vector
        def _(dve):
            def lo_static(v):
                r, half = divmod(v, 2)
                dve.wait_ge(hi_done, v + 1)
                if r in X_BLOCKS:
                    k0 = 8 * X_BLOCKS.index(r) + 4 * half
                    src = raw[:, r % RING, half * HALF:(half + 1) * HALF].rearrange("p (k s) -> p k s", s=S)
                    dve.tensor_tensor(act_t[:, k0:k0 + 4, 1, :], src, act_t[:, k0:k0 + 4, 0, :],
                                      ALU.subtract).then_inc(lo_done, 1)
                    return
                w = ring_index(v)
                n = W_IN if r < R_QIDX else HALF
                dve.tensor_tensor(w_lo[:, w % RING, 0:n], raw[:, r % RING, half * n:(half + 1) * n],
                                  w_hi[:, w % RING, 0:n], ALU.subtract).then_inc(lo_done, 1)

            def combine(m, dst):
                dve.wait_ge(low_done, m + 1)
                dve.tensor_tensor(dst, acc[:, m % 4, 0:S], low[:, m % 2, :], ALU.add).then_inc(comb_done, 1)

            for v in range(2 * R_QIDX + 2):
                lo_static(v)

            dve.wait_ge(ssq_done, 4)
            for n, width in enumerate((Q_RANK, KV_RANK)):
                dve.tensor_scalar(rstd4[:, n:4:2], ssq[:, n:4:2], 1.0 / width, EPS, ALU.mult, ALU.add)\
                   .then_inc(rms_var, 1)
            dve.wait_ge(rms_sqrt, 1)
            dve.reciprocal(rstd4, rms_v).then_inc(rms_inv, 1)
            dve.wait_ge(rms_inv, 1)
            for t in range(TOK):
                dve.tensor_scalar(proj[:, t, 0:Q_RANK], acc[:, 2 * t, :], rstd4[:, 2 * t:2 * t + 1], None,
                                  ALU.mult).then_inc(proj_done, 1)
            for n in range(KQ + KV):
                dve.wait_ge(c_hi, (n | 1) + 1)
                hi_, lo_ = (cq_t[:, n, 0, :], cq_t[:, n, 1, :]) if n < KQ else \
                    (ckv_t[:, n - KQ, 0, :], ckv_t[:, n - KQ, 1, :])
                dve.scalar_tensor_tensor(out=lo_, in0=tp[:, n // 2, (n % 2) * S:(n % 2 + 1) * S],
                                         scalar=rms_g[:, n:n + 1], in1=hi_, op0=ALU.mult,
                                         op1=ALU.subtract).then_inc(c_lo, 1)
            lo_static(2 * R_QIDX + 2)
            lo_static(2 * R_QIDX + 3)
            for m in range(M_GROUP):
                combine(m, qidx_t[:, m, :])
                if m % 2 == 1:
                    lo_static(2 * R_GROUP + m // 2)

            w0 = Q_RANK + KV_RANK + 2 * IDX_DIM
            blocks = ((0, slice(0, P)), (1, slice(P, KEYS)))
            for h in range(IDX_HEADS):
                dve.wait_ge(relu_done, h + 1)
                for t, cols in blocks:
                    w_idx = proj[:, t, w0 + h:w0 + h + 1]
                    if h == 0:
                        dve.tensor_scalar(score[:, cols], relu[:, 0, cols], w_idx, None, ALU.mult)\
                           .then_inc(score_step, 1)
                    else:
                        dve.wait_ge(score_step, 2 * (h - 1) + t + 1)
                        dve.scalar_tensor_tensor(out=score[:, cols], in0=relu[:, h % 2, cols], scalar=w_idx,
                                                 in1=score[:, cols], op0=ALU.mult, op1=ALU.add)\
                           .then_inc(score_step, 1)

            def piece(s):
                g, j = divmod(s, 4)
                m0 = M_GROUP + g * M_PER_GROUP
                if j < 2:
                    for n in range(2):
                        combine(m0 + 2 * j + n, q_t[:, g % 2, 2 * j + n, :])
                elif j == 2:
                    for n in range(GH):
                        combine(m0 + GH + n, k_t[:, g % 2, n, :])
                else:
                    for t in range(TOK):
                        m = m0 + 2 * GH + t
                        dve.wait_ge(low_done, m + 1)
                        dve.tensor_copy(v_n[:, g % 2, t, S:2 * S], acc[:, m % 4, S:2 * S]).then_inc(comb_done, 1)

            dve.wait_ge(score_masked, 2)
            for n in range(TOPK // 8):
                src = score if n == 0 else work
                if n > 0:
                    dve.wait_ge(top_step, 4 * n)
                for t, cols in blocks:
                    dve.max(top8[:, t, :], src[:, cols]).then_inc(top_step, 1)
                for t, cols in blocks:
                    dve.wait_ge(top_step, 4 * n + t + 1)
                    dve.match_replace(work[:, cols], top8[:, t, :], src[:, cols], TAKEN).then_inc(top_step, 1)
                if n % 2 == 0:
                    piece(n // 2)
                else:
                    lo_static(2 * R_GROUP + 4 + n // 2)
            dve.wait_ge(top_step, 4 * (TOPK // 8))
            dve.tensor_tensor(key_bias[:], work[:], score[:], ALU.is_equal).then_inc(bias_raw, 1)
            dve.wait_ge(bias_raw, 1)
            dve.tensor_scalar(key_bias[:], key_bias[:], MASKED, None, ALU.mult).then_inc(bias_raw, 1)
            dve.wait_ge(bias_done, 2)

            for s in range(HEADS + 2):
                if s + 4 < HEADS:
                    piece(s + 4)
                    lo_static(2 * R_GROUP + 8 + s)
                if s < HEADS:
                    dve.wait_ge(qk_full, s + 1)
                    if s >= 2:
                        dve.wait_ge(exp_done, 2 * (s - 1))
                    dve.scalar_tensor_tensor(out=neg_s[:, s % 2, :], in0=tp[:, s % 2, 0:KEYS],
                                             scalar=-ATTN_SCALE, in1=key_bias[:], op0=ALU.mult,
                                             op1=ALU.add).then_inc(neg_done, 1)
                    dve.wait_ge(neg_done, s + 1)
                    for t, cols in blocks:
                        dve.tensor_reduce(row_min[:, s % 2, t:t + 1], neg_s[:, s % 2, cols], AX.X, ALU.min)\
                           .then_inc(min_done, 1)
                if s >= 2:
                    dve.wait_ge(o_hi, s - 1)
                    dve.tensor_tensor(o_t[:, s - 2, 1, :], tp[:, 3, (s % 2) * S:(s % 2 + 1) * S],
                                      o_t[:, s - 2, 0, :], ALU.subtract).then_inc(o_lo, 1)
                if s < HEADS:
                    dve.wait_ge(exp_done, 2 * s + 2)
                    dve.reciprocal(row_inv[:, s % 2, :], row_sum[:, s % 2, :]).then_inc(inv_done, 1)
                    dve.wait_ge(inv_done, s + 1)
                    for t, cols in blocks:
                        dve.tensor_scalar(prob[:, s % 2, cols], prob[:, s % 2, cols],
                                          row_inv[:, s % 2, t:t + 1], None, ALU.mult).then_inc(prob_done, 1)

            def lo_loop(v, half, slot, n=HALF, first=None):
                first = half * n if first is None else first
                dve.wait_ge(hi_done, v + 1)
                h = (2 * slot + half) % RING
                dve.tensor_tensor(w_lo[:, h, 0:n], raw[:, slot, first:first + n], w_hi[:, h, 0:n],
                                  ALU.subtract).then_inc(lo_done, 1)

            def combine_loop(m, bank, c):
                dve.wait_ge(low_done, m + 1)
                dve.tensor_tensor(comb[:, c % 2, :], acc[:, bank, 0:S], low[:, c % 2, :], ALU.add)\
                   .then_inc(comb_done, 1)

            def residual(n, bank, tile):
                col = bass.ds(tile * P, P)
                dve.wait_ge(m_tp, n + 1)
                dve.scalar_tensor_tensor(out=xn[:, :, col], in0=xn[:, :, col], scalar=ALPHA,
                                         in1=tp[:, bank, 0:S].rearrange("p (t s) -> p t s", t=TOK),
                                         op0=ALU.mult, op1=ALU.add).then_inc(res_done, 1)
                dve.wait_ge(res_done, n + 1)
                for t in range(TOK):
                    dve.bn_stats(stats[:, t, bass.ds(tile * 6, 6)], xn[:, t, col]).then_inc(stat_done, 1)

            dve.wait_ge(xn_full, 16)

            def out_tile(c, i, with_residual=True):
                tile = RING * i + c
                for half in (0, 1):
                    lo_loop(2 * R_OUT + 2 * tile + half, half, c)
                combine_loop(M_OUT + tile - 2, (c - 2) % 4, c)
                if with_residual:
                    residual(tile - 3, (c - 3) % 4, tile - 3)

            out_tile(2, 0, with_residual=False)
            out_tile(3, 0)
            with dve.Fori(1, KD // RING) as i:
                for c in range(RING):
                    out_tile(c, i)
            for c in range(2):
                for half in (0, 1):
                    lo_loop(2 * (R_FFN + c) + half, half, c)
                combine_loop(M_OUT + KD - 2 + c, 2 + c, c)
                residual(KD - 3 + c, (KD - 3 + c) % 4, KD - 3 + c)
            residual(KD - 1, (KD - 1) % 4, KD - 1)

            def row_stats(which):
                dve.wait_ge(stat_done, TOK * KD * which)
                for t in range(TOK):
                    dve.bn_aggr(mean_var[:, 2 * t:2 * t + 2], stats[:, t, :])\
                       .then_inc(aggr_done, 1)
                dve.wait_ge(aggr_done, TOK * which)
                dve.tensor_scalar(ln_v, mean_var[:, 1:4:2], EPS, None, ALU.add).then_inc(var_done, 1)
                dve.wait_ge(sqrt_done, which)
                dve.reciprocal(ln_r, ln_s).then_inc(rstd_done, 1)
                dve.wait_ge(rstd_done, which)

            row_stats(1)
            for c in range(4):
                for t in range(TOK):
                    part = xn[:, t, c * 512:(c + 1) * 512]
                    dve.tensor_scalar(part, part, mean_var[:, 2 * t:2 * t + 1], ln_r[:, t:t + 1],
                                      ALU.subtract, ALU.mult).then_inc(xhat_done, 1)
            vals = (low, comb)
            for k in range(KD):
                dve.wait_ge(xt_hi, (k | 1) + 1)
                if k >= 4:
                    dve.wait_ge(xt_lo, k - 3)
                dve.tensor_scalar(vals[(k // 2) % 2][:, k % 2, :],
                                  tp[:, (k // 2) % 4, (k % 2) * S:(k % 2 + 1) * S],
                                  ln1_gb[:, 0, k:k + 1], ln1_gb[:, 1, k:k + 1], ALU.mult, ALU.add)\
                   .then_inc(xt_val, 1)

            def ffn_combine(tile, c):
                dve.wait_ge(ffn_low, tile + 1)
                dve.tensor_tensor(comb[:], acc[:, 2 * c:2 * c + 2, 0:S], low[:], ALU.add).then_inc(ffn_comb, 1)

            def ffn_mul(tile):
                dve.wait_ge(ffn_sig, tile + 1)
                dve.tensor_tensor(hid[:], sig[:], comb[:, 1, :], ALU.mult).then_inc(ffn_hid, 1)

            def ffn_lo_step(tile):
                dve.wait_ge(ffn_hi, tile + 1)
                dve.tensor_tensor(hid_flat[:, bass.ds(tile * 2 * S + S, S)], hid[:],
                                  hid_flat[:, bass.ds(tile * 2 * S, S)], ALU.subtract).then_inc(ffn_lo, 1)

            def ffn_tile(c, i, older=True):
                tile = 2 * i + c
                for j in range(4):
                    lo_loop(2 * R_FFN + 4 * tile + j, j % 2, 2 * c + j // 2)
                    if j == 0 and older:
                        ffn_mul(tile - 2)
                    if j == 1 and older:
                        ffn_lo_step(tile - 2)
                ffn_combine(tile - 1, 1 - c)

            ffn_tile(1, 0, older=False)
            with dve.Fori(1, KF // 2) as i:
                ffn_tile(0, i)
                ffn_tile(1, i)

            def down_half(j, i):
                lo_loop(2 * R_DOWN + 8 * i + j, j % 2, j // 2, n=DOWN_K[j] * P, first=(j % 2) * DOWN_K[0] * P)

            for j in range(8):
                down_half(j, 0)
                if j == 0:
                    ffn_mul(KF - 2)
                if j == 1:
                    ffn_lo_step(KF - 2)
                if j == 3:
                    ffn_combine(KF - 1, 1)
                    ffn_mul(KF - 1)
                    ffn_lo_step(KF - 1)

            def down_tile(c, i):
                prev = 2 * i + c - 1
                for j in range(8):
                    down_half(j, 2 * i + c)
                    if j == 3:
                        combine_loop(M_DOWN + prev, 1 - c, 1 - c)
                    if j == 6:
                        residual(KD + prev, 1 - c, prev)

            dve.wait_ge(x1_step, 16)
            down_tile(1, 0)
            with dve.Fori(1, KD // 2) as i:
                down_tile(0, i)
                down_tile(1, i)
            combine_loop(M_DOWN + KD - 1, 1, 1)
            residual(2 * KD - 1, 1, KD - 1)

            row_stats(2)
            dve.scalar_tensor_tensor(out=ln_nmr, in0=mean_var[:, 0:4:2], scalar=-1.0, in1=ln_r,
                                     op0=ALU.mult, op1=ALU.mult).then_inc(nmr_done, 1)
            for c in range(4):
                for t in range(TOK):
                    part = xn[:, t, c * 512:(c + 1) * 512]
                    dve.wait_ge(y_norm, 2 * c + t + 1)
                    dve.tensor_tensor(part, part, ln_rows[:, 2, c * 512:(c + 1) * 512], ALU.mult)\
                       .then_inc(y_gain, 1)

        @block.gpsimd
        def _(pool):
            pool.dma_start(rms_g[:], a["rms_g_t"]).then_inc(rms_full, 16)
            pool.memset(ident[:], 0.0).then_inc(ident_done, 1)
            pool.wait_ge(ident_done, 1)
            pool.affine_select(out=ident[:], in_=ident[:], compare_op=ALU.not_equal, fill=1.0, base=0,
                               pattern=[[-1, P]], channel_multiplier=1).then_inc(ident_done, 1)
            blocks = ((0, slice(0, P), P), (1, slice(P, KEYS), S))
            pool.wait_ge(score_step, 2 * IDX_HEADS)
            for t, cols, n in blocks:
                pool.affine_select(out=score[:, cols], in_=score[:, cols], compare_op=ALU.is_ge,
                                   fill=NOT_CAUSAL, base=t * P, pattern=[[-1, n]], channel_multiplier=1)\
                    .then_inc(score_masked, 1)
            pool.wait_ge(bias_raw, 2)
            for t, cols, n in blocks:
                pool.affine_select(out=key_bias[:, cols], in_=key_bias[:, cols], compare_op=ALU.is_ge,
                                   fill=MASKED, base=t * P, pattern=[[-1, n]], channel_multiplier=1)\
                    .then_inc(bias_done, 1)
            vals = (low, comb)
            for k in range(KD):
                pool.wait_ge(xt_hi, k + 1)
                pool.wait_ge(xt_val, k + 1)
                pool.tensor_tensor(act_t[:, k, 1, :], vals[(k // 2) % 2][:, k % 2, :], act_t[:, k, 0, :],
                                   ALU.subtract).then_inc(xt_lo, 1)
            pool.wait_ge(rows_full, 64)
            n = 0
            for c in range(4):
                for t in range(TOK):
                    part = xn[:, t, c * 512:(c + 1) * 512]
                    pool.tensor_tensor(part, part, ln_rows[:, 0, c * 512:(c + 1) * 512], ALU.mult)\
                        .then_inc(x1_step, 1)
                    n += 1
                    pool.wait_ge(x1_step, n)
                    pool.tensor_tensor(part, part, ln_rows[:, 1, c * 512:(c + 1) * 512], ALU.add)\
                        .then_inc(x1_step, 1)
                    n += 1
            for c in range(4):
                for t in range(TOK):
                    part = xn[:, t, c * 512:(c + 1) * 512]
                    pool.wait_ge(y_gain, 2 * c + t + 1)
                    pool.tensor_tensor(part, part, ln_rows[:, 3, c * 512:(c + 1) * 512], ALU.add)\
                        .then_inc(y_done, 1)

        @block.tensor
        def _(pe):
            def pair(bank, w, e0, rhs, start, stop):
                wh = w_hi[:, w, e0:e0 + P]
                wl = w_lo[:, w, e0:e0 + P]
                if start:
                    pe.matmul(acc[:, bank, :], wh, rhs, start=True, stop=False)
                    return pe.matmul(acc[:, bank, 0:S], wl, rhs[:, 0, :], start=False, stop=False,
                                     skip_group_check=True)
                pe.matmul(acc[:, bank, 0:S], wl, rhs[:, 0, :], start=False, stop=False, skip_group_check=True)
                return pe.matmul(acc[:, bank, :], wh, rhs, start=False, stop=stop)

            spans = ((0, 0, Q_RANK), (1, Q_RANK, W_IN))
            for k in range(KD):
                v = 2 * IN_BLOCKS[k // 2] + k % 2
                w = ring_index(v) % RING
                pe.wait_ge(lo_done, v + 1)
                for t in range(TOK):
                    for x_part, w_part in ((0, w_hi), (0, w_lo), (1, w_hi)):
                        for b, c0, c1 in spans:
                            last = pe.matmul(acc[:, 2 * t + b, 0:c1 - c0],
                                             act_t[:, k, x_part, t * P:(t + 1) * P], w_part[:, w, c0:c1],
                                             start=(k == 0 and x_part == 0 and w_part is w_hi),
                                             stop=(k == KD - 1 and x_part == 1))
                last.then_inc(pe_used, 1)
            pe.wait_ge(ident_done, 2)
            pe.wait_ge(proj_done, 8)
            for n in range(KQ + KV + 1):
                for t in range(TOK):
                    last = pe.transpose(tp[:, n // 2, (n % 2) * S + t * P:(n % 2) * S + (t + 1) * P],
                                        proj[:, t, n * P:(n + 1) * P], ident[:])
                last.then_inc(proj_t, 1)

            def project(v, tiles, kts, act_tiles, m0):
                w = ring_index(v) % RING
                pe.wait_ge(lo_done, v + 1)
                for n in range(tiles):
                    m = m0 + n
                    if m >= 4:
                        pe.wait_ge(comb_done, m - 3)
                    for k in range(kts):
                        last = pair(m % 4, w, (n * kts + k) * P, act_tiles[:, k, :, :], k == 0, k == kts - 1)
                    last.then_inc(acc_full, 1)

            pe.wait_ge(c_hi, KQ + KV + 1)
            pe.wait_ge(c_lo, KQ + KV)
            for half in range(4):
                project(2 * R_QIDX + half, 2, KQ, cq_t, M_QIDX + 2 * half)

            for h in range(IDX_HEADS):
                pe.wait_ge(comb_done, h // 2 + 1)
                if h >= 4:
                    pe.wait_ge(relu_done, h - 3)
                rows = slice(IDX_DIM * (h % 2), IDX_DIM * (h % 2) + IDX_DIM)
                for t, c0, n in ((0, 0, P), (1, P, S)):
                    last = pe.matmul(tp[:, h % 4, c0:c0 + n], qidx_t[rows, h // 2, t * P:(t + 1) * P],
                                     kidx_t[rows, 0:n], start=True, stop=True)
                last.then_inc(logits_full, 1)

            def piece(s):
                g, j = divmod(s, 4)
                m0 = M_GROUP + g * M_PER_GROUP
                v = 2 * R_GROUP + s
                if j < 2:
                    project(v, 2, KQ, cq_t, m0 + 2 * j)
                elif j == 2:
                    project(v, GH, KV, ckv_t, m0 + GH)
                else:
                    w = ring_index(v) % RING
                    pe.wait_ge(lo_done, v + 1)
                    for t in range(TOK):
                        m = m0 + 2 * GH + t
                        pe.wait_ge(comb_done, m - 3)
                        steps = [(k, x, wp) for k in range(KV) for x, wp in ((0, w_hi), (0, w_lo), (1, w_hi))]
                        for n, (k, x, wp) in enumerate(steps):
                            last = pe.matmul(acc[:, m % 4, :], ckv_t[:, k, x, t * P:(t + 1) * P],
                                             wp[:, w, k * 512:(k + 1) * 512], start=(n == 0),
                                             stop=(n == len(steps) - 1))
                        last.then_inc(acc_full, 1)

            for s in range(4):
                piece(s)
            pe.wait_ge(relu_done, IDX_HEADS)
            for s in range(HEADS + 2):
                if s + 4 < HEADS:
                    piece(s + 4)
                if s < HEADS:
                    g, h = divmod(s, GH)
                    pe.wait_ge(comb_done, M_GROUP + (g + 1) * M_PER_GROUP)
                    if s >= 2:
                        pe.wait_ge(neg_done, s - 1)
                    for t, c0, n in ((0, 0, P), (1, P, S)):
                        last = pe.matmul(tp[:, s % 2, c0:c0 + n], q_t[:, g % 2, h, t * P:(t + 1) * P],
                                         k_t[:, g % 2, h, 0:n], start=True, stop=True)
                    last.then_inc(qk_full, 1)
                if 1 <= s <= HEADS:
                    u = s - 1
                    pe.wait_ge(prob_done, 2 * u + 2)
                    if u >= 1:
                        pe.wait_ge(pt_done, u)
                    for n in range(KEYS // P):
                        last = pe.transpose(tp[:, 2, n * P:(n + 1) * P], prob[:, u % 2, n * P:(n + 1) * P],
                                            ident[:])
                    last.then_inc(pt_full, 1)
                if s >= 2:
                    u = s - 2
                    g, h = divmod(u, GH)
                    pe.wait_ge(pt_done, u + 1)
                    if u >= 1:
                        pe.wait_ge(o_lo, u)
                    c0 = (u % 2) * S
                    v_h = [v_n[:, g % 2, t, h * HD:(h + 1) * HD] for t in range(TOK)]
                    pe.matmul(tp[:, 3, c0:c0 + P], v_h[0], prob_t[:, u % 2, 0:P], start=True, stop=True)
                    pe.matmul(tp[:, 3, c0 + P:c0 + S], v_h[0], prob_t[:, u % 2, P:2 * P], start=True, stop=False)
                    pe.matmul(tp[:, 3, c0 + P:c0 + S], v_h[1], prob_t[:, u % 2, 2 * P:3 * P], start=False,
                              stop=True).then_inc(pv_full, 1)

            def turn(n, bank, c):
                for t in range(TOK):
                    last = pe.transpose(tp[:, bank, t * P:(t + 1) * P], comb[:, c, t * P:(t + 1) * P], ident[:])
                last.then_inc(m_tp, 1)

            pe.wait_ge(o_lo, HEADS)

            def out_tile(c, i, prev=True):
                tile = RING * i + c
                pe.wait_ge(comb_done, M_OUT + tile - 3)
                for half in (0, 1):
                    pe.wait_ge(lo_done, 2 * R_OUT + 2 * tile + half + 1)
                    for n in range(8):
                        k = 8 * half + n
                        last = pair(c, (2 * c + half) % RING, n * P, o_t[:, k, :, :], k == 0, k == KD - 1)
                    last.then_inc(*((pe_used, 1) if half == 0 else (acc_full, 1)))
                if prev:
                    pe.wait_ge(comb_done, M_OUT + tile)
                    if not (isinstance(i, int) and tile <= 4):
                        pe.wait_ge(res_done, tile - 4)
                    turn(tile - 1, (c - 1) % 4, (c - 1) % 2)

            out_tile(0, 0, prev=False)
            for c in range(1, RING):
                out_tile(c, 0)
            out_tile(0, 1)
            for c in range(1, RING):
                out_tile(c, 1)
            with pe.Fori(2, KD // RING) as i:
                for c in range(RING):
                    out_tile(c, i)
            pe.wait_ge(comb_done, M_OUT + KD)
            turn(KD - 1, 3, 1)

            for k in range(KD):
                if k % 4 == 0:
                    pe.wait_ge(xhat_done, 2 * (k // 4) + 2)
                if k % 2 == 0 and k >= 8:
                    pe.wait_ge(xt_hi, k - 6)
                    pe.wait_ge(xt_val, k - 6)
                for t in range(TOK):
                    c0 = (k % 2) * S + t * P
                    last = pe.transpose(tp[:, (k // 2) % 4, c0:c0 + P], xn[:, t, k * P:(k + 1) * P], ident[:])
                last.then_inc(xt_full, 1)

            def ffn_tile(c, i, first=False):
                tile = 2 * i + c
                if not (isinstance(i, int) and i == 0):
                    pe.wait_ge(ffn_comb, tile - 1)
                for j in range(4):
                    pe.wait_ge(lo_done, 2 * R_FFN + 4 * tile + j + 1)
                    for n in range(8):
                        k = 8 * (j % 2) + n
                        if first:
                            pe.wait_ge(xt_lo, k + 1)
                        last = pair(2 * c + j // 2, j, n * P, act_t[:, k, :, :], k == 0, k == KD - 1)
                    last.then_inc(*((pe_used, 1) if j < 3 else (ffn_full, 1)))

            ffn_tile(0, 0, first=True)
            ffn_tile(1, 0)
            with pe.Fori(1, KF // 2) as i:
                ffn_tile(0, i)
                ffn_tile(1, i)

            def down_tile(c, i, first=False, second=False):
                tile = 2 * i + c
                if first:
                    pe.wait_ge(ffn_comb, KF - 1)
                elif second:
                    pe.wait_ge(ffn_comb, KF)
                else:
                    pe.wait_ge(comb_done, M_DOWN + tile - 1)
                k = 0
                for j in range(8):
                    pe.wait_ge(lo_done, 2 * R_DOWN + 8 * tile + j + 1)
                    if first and j in (0, 7):
                        pe.wait_ge(ffn_lo, KF if j == 7 else KF - 2)
                    for n in range(DOWN_K[j]):
                        last = pair(c, j % RING, n * P, hid_t[:, k, :, :], k == 0, k == KF - 1)
                        k += 1
                    last.then_inc(*((pe_used, 1) if j < 7 else (acc_full, 1)))
                    if j == 2 and not first:
                        pe.wait_ge(comb_done, M_DOWN + tile)
                        if not second:
                            pe.wait_ge(res_done, KD + tile - 2)
                        turn(KD + tile - 1, 1 - c, 1 - c)

            down_tile(0, 0, first=True)
            down_tile(1, 0, second=True)
            with pe.Fori(1, KD // 2) as i:
                down_tile(0, i)
                down_tile(1, i)
            pe.wait_ge(comb_done, M_DOWN + KD)
            turn(2 * KD - 1, 1, 1)


_OUT = ((1, S, D), "float32")


def kernel(**inputs):
    from concourse import bacc
    from concourse.bass_utils import run_bass_kernel_spmd

    w = {n: np.asarray(v) for n, v in inputs.items()}

    def k_tiles(m, cols):
        k, n = m.shape
        return m.reshape(k // P, P, n // cols, cols).transpose(2, 1, 0, 3).reshape(n // cols, P, -1)

    x = w["x"].reshape(S, D)
    uq = k_tiles(w["l0_w_uq"], P).reshape(GROUPS, GH, P, -1).transpose(0, 2, 1, 3).reshape(GROUPS, P, -1)
    uk = w["l0_w_uk"].reshape(GROUPS, GH, HD, KV, P).transpose(0, 4, 1, 3, 2).reshape(GROUPS, P, -1)
    uv = w["l0_w_uv"].reshape(GROUPS, GH, KV, P, HD).transpose(0, 3, 2, 1, 4).reshape(GROUPS, P, -1)
    gate, up = (k_tiles(w[n], P) for n in ("l0_ffn_gate", "l0_ffn_up"))
    down = k_tiles(w["l0_ffn_down"], P).reshape(KD, P, 4, 11 * P).transpose(0, 2, 1, 3)
    arrays = {
        "x": x,
        "x_t": x.T.reshape(2, 8, P, S).transpose(0, 2, 1, 3).reshape(2, P, -1),
        "w_in": w["l0_w_in"].reshape(8, 2, P, W_IN).transpose(0, 2, 1, 3).reshape(8, P, -1),
        "w_qidx": k_tiles(w["l0_w_qidx"], P).reshape(2, 4, P, -1).transpose(0, 2, 1, 3).reshape(2, P, -1),
        "w_uq": uq,
        "w_ukv": np.concatenate([uk, uv], axis=2),
        "w_out": k_tiles(w["l0_w_out"], P),
        "w_gu": np.stack([gate, up], axis=1).reshape(2 * KF, P, -1),
        "w_down": down.reshape(4 * KD, P, -1),
        "rms_g_t": np.concatenate([w["l0_q_norm"].reshape(KQ, P), w["l0_kv_norm"].reshape(KV, P)]).T,
        "ln1_gb_t": np.stack([w["l0_ln1_g"], w["l0_ln1_b"]]).reshape(2, KD, P).transpose(2, 0, 1),
        "ln_rows": np.stack([w["l0_ln1_g"], w["l0_ln1_b"], w["l0_ln2_g"], w["l0_ln2_b"]]),
    }
    nc = bacc.Bacc("TRN2", target_bir_lowering=False, num_devices=1)
    feed, aps = {}, {}
    for name, value in arrays.items():
        value = np.ascontiguousarray(value)
        feed["in_" + name] = value
        aps[name] = nc.dram_tensor("in_" + name, value.shape, mybir.dt.from_np(value.dtype),
                                   kind="ExternalInput").ap()
    aps["out"] = nc.dram_tensor("out_0", (S, D), F32, kind="ExternalOutput").ap()
    layer_kernel(nc, aps)
    r = run_bass_kernel_spmd(nc, [feed], core_ids=[0])
    return r.results[0]["out_0"].reshape(_OUT[0])
```

```python
from contextlib import ExitStack

import numpy as np

import concourse.bass as bass
from concourse import mybir

F32 = mybir.dt.float32
F32R = mybir.dt.float32r
ACT = mybir.ActivationFunctionType
ALU = mybir.AluOpType
AX = mybir.AxisListType

P = 128
D = 2048
S = 256
TOK = S // P
KD = D // P
Q_RANK = 512
KV_RANK = 256
IDX_DIM = 64
IDX_HEADS = 16
HEADS = 16
HD = 128
TOPK = min(256, S // 4)
FFN = 5632
KF = FFN // P
ALPHA = 2.0 ** 0.25
EPS = 1e-5
ATTN_SCALE = HD ** -0.5
IDX_SCALE = (IDX_HEADS ** -0.5) * (IDX_DIM ** -0.5)
W_IN = Q_RANK + KV_RANK + IDX_DIM + IDX_HEADS
KQ = Q_RANK // P
KV = KV_RANK // P
GH = 4
GROUPS = HEADS // GH
KEYS = S + P
MASKED = 1e30
NOT_CAUSAL = -3.0e38
TAKEN = -3.4e38
NOT_TAKEN = -3.2e38

RAW_ELEMS = 2048
HALF = RAW_ELEMS // 2
RING = 4
X_BLOCKS = (0, 2)
IN_BLOCKS = (1, 3, 4, 5, 6, 7, 8, 9)
R_QIDX = 10
R_GROUP = 12
R_OUT = R_GROUP + 2 * GROUPS
R_FFN = R_OUT + KD
R_DOWN = R_FFN + 2 * KF
POOL_LO = (1, 5, 9, 13)
POOL_NORM = HEADS - GH
RELU = 3
Y_SHARED = ((0, 0), (0, 1), (1, 0), (2, 0), (3, 0))
Y_OWN = ((1, 1), (2, 1), (3, 1))
Y_ORDER = ((1, 0), (0, 0), (0, 1), (1, 1), (0, 2), (0, 3), (0, 4), (1, 2))
ACT_XHAT = 3
DOWN_K = (6, 5) * 4

M_QIDX = 0
M_GROUP = M_QIDX + IDX_HEADS * IDX_DIM // P
M_PER_GROUP = 2 * GH + TOK
M_OUT = M_GROUP + GROUPS * M_PER_GROUP
M_DOWN = M_OUT + KD


SPLIT_ORDER = (0, 2, 3, 1)
SPLIT_PLACE = {v: n for n, v in enumerate(SPLIT_ORDER)}


def ring_index(v):
    x_before = sum(1 for b in X_BLOCKS for h in (0, 1) if 2 * b + h < v)
    return v - x_before


def layer_kernel(nc, a):
    ctx = ExitStack()
    with ctx:
        def sb(name, shape, dt=F32):
            return ctx.enter_context(nc.sbuf_tensor(name, shape, dt))

        def sem(name):
            return ctx.enter_context(nc.semaphore(name))

        raw = sb("raw", [P, RING, RAW_ELEMS])
        w_hi = sb("w_hi", [P, RING, HALF], F32R)
        w_lo = sb("w_lo", [P, RING, HALF], F32R)
        base_a = nc.sbuf_base
        act_t = sb("act_t", [P, KD, 2, S], F32R)
        base_r = nc.sbuf_base
        hid_t = sb("hid_t", [P, KF, 2, S], F32R)
        xn = sb("xn", [P, TOK, D])
        ident = sb("ident", [P, P])
        low = sb("low", [P, 2, S])
        comb = sb("comb", [P, 2, S])
        sig = sb("sig", [P, S])
        hid = sb("hid", [P, S])
        stats = sb("stats", [P, TOK, KD * 6])
        small = sb("small", [P, 28])
        ln1_gb = sb("ln1_gb", [P, 2, KD])

        def at(base):
            offset = [base]

            def place(name, shape, dt=F32):
                t = nc.alloc_sbuf_tensor_at(name, shape, dt, offset=offset[0])
                offset[0] += int(np.prod(shape[1:])) * 4
                return t
            return place

        place = at(base_a)
        q_t = place("q_t", [P, 2, GH, S])
        k_t = place("k_t", [P, 2, GH, S])
        v_n = place("v_n", [P, 2, TOK, GH * HD])
        score = place("score", [P, KEYS])
        work = place("work", [P, KEYS])
        key_bias = place("key_bias", [P, KEYS])
        top8 = place("top8", [P, TOK, 8])
        place = at(base_r)
        o_t = place("o_t", [P, HEADS, 2, S], F32R)
        PROJ = Q_RANK + KV_RANK + 2 * IDX_DIM + IDX_HEADS
        proj = place("proj", [P, TOK, PROJ])
        cq_t = place("cq_t", [P, KQ, 2, S], F32R)
        ckv_t = place("ckv_t", [P, KV, 2, S], F32R)
        kidx_t = place("kidx_t", [P, S])
        qidx_t = place("qidx_t", [P, IDX_HEADS * IDX_DIM // P, S])
        relu = place("relu", [P, RELU, KEYS])
        neg_s = place("neg_s", [P, 2, KEYS])
        prob = place("prob", [P, 3, KEYS])
        prob_t = place("prob_t", [P, 2, KEYS])
        sq = place("sq", [P, Q_RANK])
        rms_g = place("rms_g", [P, KQ + KV])
        ln1_rows = at(base_r + (KF * 2 * S - 2 * D) * 4)("ln1_rows", [P, 2, D])
        ln2_rows = at(base_a)("ln2_rows", [P, 2, D])

        ssq = small[:, 0:4]
        rms_v = small[:, 4:8]
        rstd4 = small[:, 8:12]
        rms_r = small[:, 24:28]
        mean_var = small[:, 12:16]
        ln_v = small[:, 16:18]
        ln_s = small[:, 18:20]
        ln_r = small[:, 20:22]
        ln_nmr = small[:, 22:24]
        table_in = sb("table_in", [P, 2])
        row_min = sb("row_min", [P, 2, TOK])
        row_sum = sb("row_sum", [P, 2, TOK])
        row_inv = sb("row_inv", [P, 2, TOK])

        acc = ctx.enter_context(nc.psum_tensor("acc", [P, 4, 512], F32))
        tp = ctx.enter_context(nc.psum_tensor("tp", [P, 4, 512], F32))

        raw_full = [sem(f"raw_full{i}") for i in range(RING)]
        first_full = [sem(f"first_full{i}") for i in range(2)]
        const_full = sem("const_full")
        table_set = sem("table_set")
        rms_full = sem("rms_full")
        xn_full = sem("xn_full")
        ln1_rows_full = sem("ln1_rows_full")
        ln2_rows_full = sem("ln2_rows_full")
        out_done = sem("out_done")
        hi_done = sem("hi_done")
        lo_done = sem("lo_done")
        pe_used = sem("pe_used")
        ident_done = sem("ident_done")
        ssq_done = sem("ssq_done")
        rms_var = sem("rms_var")
        rms_sqrt = sem("rms_sqrt")
        rms_inv = sem("rms_inv")
        proj_done = sem("proj_done")
        proj_q_done = sem("proj_q_done")
        proj_t = sem("proj_t")
        c_hi = sem("c_hi")
        c_lo = sem("c_lo")
        acc_full = sem("acc_full")
        low_done = sem("low_done")
        comb_done = sem("comb_done")
        logits_full = sem("logits_full")
        relu_done = sem("relu_done")
        score_step = sem("score_step")
        score_masked = sem("score_masked")
        top_step = sem("top_step")
        bias_raw = sem("bias_raw")
        bias_done = sem("bias_done")
        qk_full = sem("qk_full")
        neg_done = sem("neg_done")
        min_done = sem("min_done")
        exp_done = sem("exp_done")
        inv_done = sem("inv_done")
        prob_done = sem("prob_done")
        pt_full = sem("pt_full")
        pt_done = sem("pt_done")
        pv_full = sem("pv_full")
        o_hi = sem("o_hi")
        o_lo = sem("o_lo")
        m_tp = sem("m_tp")
        res_done = sem("res_done")
        stat_done = sem("stat_done")
        aggr_done = sem("aggr_done")
        var_done = sem("var_done")
        sqrt_done = sem("sqrt_done")
        rstd_done = sem("rstd_done")
        xhat_done = sem("xhat_done")
        xhat_act = sem("xhat_act")
        xt_full = sem("xt_full")
        xt_hi = sem("xt_hi")
        xt_val = sem("xt_val")
        xt_lo = sem("xt_lo")
        xt_lo_pool = sem("xt_lo_pool")
        ffn_full = sem("ffn_full")
        ffn_low = sem("ffn_low")
        ffn_comb = sem("ffn_comb")
        ffn_sig = sem("ffn_sig")
        ffn_hid = sem("ffn_hid")
        ffn_hi = sem("ffn_hi")
        ffn_lo = sem("ffn_lo")
        x1_step = sem("x1_step")
        nmr_done = sem("nmr_done")
        y_norm = sem("y_norm")
        y_gain = sem("y_gain")
        y_done = sem("y_done")
        y_scaled = sem("y_scaled")
        y_own_done = sem("y_own_done")

        block = ctx.enter_context(nc.Block())

        in_raw = {b: n for n, b in enumerate(IN_BLOCKS)}
        hid_flat = hid_t[:].rearrange("p k h s -> p (k h s)")

        def flat(name):
            return a[name].rearrange("n p e -> (n p) e")

        w_out_rows, w_gu_rows, w_down_rows = flat("w_out"), flat("w_gu"), flat("w_down")

        def used_out(tile, half):
            return (pe_used, KD + tile + 1) if half == 0 else (acc_full, M_OUT + tile + 1)

        def used_ffn(tile, j):
            return (pe_used, 2 * KD + 3 * tile + j + 1) if j < 3 else (ffn_full, tile + 1)

        def used_down(tile, j):
            return (pe_used, 2 * KD + 3 * KF + 7 * tile + j + 1) if j < 7 else (acc_full, M_DOWN + tile + 1)

        def used_static(v):
            if v < 2 * R_QIDX:
                return pe_used, sum(1 for b in IN_BLOCKS for h in (0, 1) if 2 * b + h <= v)
            if v < 2 * R_GROUP:
                return acc_full, 2 * (v - 2 * R_QIDX) + 2
            if v < 2 * R_OUT:
                g, j = divmod(v - 2 * R_GROUP, 4)
                return acc_full, M_GROUP + g * M_PER_GROUP + (2, 4, 8, 10)[j]
            return used_out(*divmod(v - 2 * R_OUT, 2))

        @block.sync
        def _(sp):
            def load(r, slot, dst_elems, src, first=False, late=0):
                if not first:
                    sp.wait_ge(lo_done, len(SPLIT_ORDER) if isinstance(r, int) and r == 4 else 2 * r - 6 + late)
                sp.dma_start(raw[:, slot, 0:dst_elems], src).then_inc(raw_full[slot], 16)

            for v in SPLIT_ORDER:
                r, half = divmod(v, 2)
                src = a["x_t"][0] if r in X_BLOCKS else a["w_in"][0]
                n = HALF if r in X_BLOCKS else W_IN
                full = raw_full[r] if half == 1 else first_full[r]
                sp.dma_start(raw[:, r, half * n:(half + 1) * n], src[:, half * n:(half + 1) * n])\
                    .then_inc(full, 16)

            def rows(dst, first, full):
                for n in range(2):
                    row = a["ln_rows"][first + n:first + n + 1, :].broadcast_to([P, D])
                    sp.dma_start(dst[:, n, :], row).then_inc(full, 16)

            for r in range(len(SPLIT_ORDER) // 2, R_QIDX):
                if r in X_BLOCKS:
                    load(r, r % RING, RAW_ELEMS, a["x_t"][X_BLOCKS.index(r)], first=r < RING)
                else:
                    load(r, r % RING, 2 * W_IN, a["w_in"][in_raw[r]], first=r < RING)
            for n in range(2):
                load(R_QIDX + n, (R_QIDX + n) % RING, RAW_ELEMS, a["w_qidx"][n])
            for g in range(GROUPS):
                r = R_GROUP + 2 * g
                load(r, r % RING, RAW_ELEMS, a["w_uq"][g])
                load(r + 1, (r + 1) % RING, RAW_ELEMS, a["w_ukv"][g])
                if g == 0:
                    sp.dma_start(xn[:], a["x"].rearrange("(t p) d -> p t d", p=P)).then_inc(xn_full, 16)
            with sp.Fori(0, KD // RING) as i:
                for j in range(RING):
                    load(R_OUT + i * RING + j, j, RAW_ELEMS, w_out_rows[bass.ds((i * RING + j) * P, P), :])
            sp.wait_ge(pv_full, HEADS)
            rows(ln1_rows, 0, ln1_rows_full)
            with sp.Fori(0, KF // 2) as i:
                for j in range(RING):
                    load(R_FFN + i * RING + j, j, RAW_ELEMS, w_gu_rows[bass.ds((i * RING + j) * P, P), :],
                         late=1)
            for n in range(RING):
                load(R_DOWN + n, n, 11 * P, a["w_down"][n])
            sp.wait_ge(ffn_full, KF)
            rows(ln2_rows, 2, ln2_rows_full)
            with sp.Fori(1, KD) as i:
                for j in range(RING):
                    load(R_DOWN + i * RING + j, j, 11 * P, w_down_rows[bass.ds((i * RING + j) * P, P), :])
            for own, n in Y_ORDER:
                if own:
                    sp.wait_ge(y_own_done, n + 1)
                else:
                    sp.wait_ge(y_done, n + 1)
                c, t = (Y_OWN if own else Y_SHARED)[n]
                sp.dma_start(a["out"][t * P:(t + 1) * P, c * 512:(c + 1) * 512],
                             xn[:, t, c * 512:(c + 1) * 512]).then_inc(out_done, 16)
            sp.wait_ge(out_done, 16 * 8)

        @block.scalar
        def _(act):
            act.wait_ge(table_set, 1)
            act.dma_start(ln1_gb[:], a["ln1_gb_t"]).then_inc(const_full, 16)

            def hi_static(v):
                r, half = divmod(v, 2)
                if v in SPLIT_ORDER:
                    act.wait_ge(raw_full[r] if half == 1 else first_full[r], 16)
                elif half == 0:
                    act.wait_ge(raw_full[r % RING], 16 * (r // RING + 1))
                if r in X_BLOCKS:
                    k0 = 8 * X_BLOCKS.index(r) + 4 * half
                    src = raw[:, r % RING, half * HALF:(half + 1) * HALF].rearrange("p (k s) -> p k s", s=S)
                    act.activation(act_t[:, k0:k0 + 4, 0, :], src, ACT.Copy).then_inc(hi_done, 1)
                    return
                w = ring_index(v)
                if w >= RING:
                    prev = next(u for u in range(v) if ring_index(u) == w - RING and u // 2 not in X_BLOCKS)
                    act.wait_ge(*used_static(prev))
                n = W_IN if r < R_QIDX else HALF
                act.activation(w_hi[:, w % RING, 0:n], raw[:, r % RING, half * n:(half + 1) * n],
                               ACT.Copy).then_inc(hi_done, 1)

            def take_low(m):
                act.wait_ge(acc_full, m + 1)
                if m >= 2:
                    act.wait_ge(comb_done, m - 1)
                act.activation(low[:, m % 2, :], acc[:, m % 4, S:2 * S], ACT.Copy).then_inc(low_done, 1)

            def load_table(func):
                act.activation(table_in[:, 1:2], table_in[:, 0:1], func)

            for v in SPLIT_ORDER + tuple(range(len(SPLIT_ORDER), 2 * R_QIDX)):
                hi_static(v)
            hi_static(2 * R_QIDX)
            hi_static(2 * R_QIDX + 1)

            load_table(ACT.Sqrt)
            act.wait_ge(pe_used, KD)
            for t in range(TOK):
                act.activation(sq[:, 0:Q_RANK], acc[:, 2 * t, :], ACT.Square,
                               accum_out=ssq[:, 2 * t:2 * t + 1]).then_inc(ssq_done, 1)
                act.wait_ge(ssq_done, 2 * t + 1)
                act.activation(sq[:, 0:KV_RANK], acc[:, 2 * t + 1, 0:KV_RANK], ACT.Square,
                               accum_out=ssq[:, 2 * t + 1:2 * t + 2]).then_inc(ssq_done, 1)
                act.wait_ge(ssq_done, 2 * t + 2)
            act.wait_ge(rms_var, 2)
            act.activation(rms_v, rstd4, ACT.Sqrt).then_inc(rms_sqrt, 1)
            for t in range(TOK):
                c = Q_RANK + KV_RANK
                act.activation(proj[:, t, c:c + IDX_DIM], acc[:, 2 * t + 1, KV_RANK:KV_RANK + IDX_DIM],
                               ACT.Copy).then_inc(proj_done, 1)
                act.activation(proj[:, t, c + IDX_DIM:c + 2 * IDX_DIM + IDX_HEADS],
                               acc[:, 2 * t + 1, KV_RANK:KV_RANK + IDX_DIM + IDX_HEADS],
                               ACT.Copy).then_inc(proj_done, 1)
            act.wait_ge(rms_inv, 4)
            for t in range(TOK):
                act.activation(proj[:, t, Q_RANK:Q_RANK + KV_RANK], acc[:, 2 * t + 1, 0:KV_RANK], ACT.Copy,
                               scale=rstd4[:, 2 * t + 1:2 * t + 2]).then_inc(proj_done, 1)
            act.wait_ge(rms_full, 16)
            act.wait_ge(const_full, 16)
            for n in range(KQ + KV):
                act.wait_ge(proj_t, (n | 1) + 1)
                dst = cq_t[:, n, 0, :] if n < KQ else ckv_t[:, n - KQ, 0, :]
                act.activation(dst, tp[:, n // 2, (n % 2) * S:(n % 2 + 1) * S], ACT.Copy,
                               scale=rms_g[:, n:n + 1]).then_inc(c_hi, 1)
            act.wait_ge(proj_t, KQ + KV + 1)
            act.activation(kidx_t[:], tp[:, 3, 0:S], ACT.Copy).then_inc(c_hi, 1)
            hi_static(2 * R_QIDX + 2)
            hi_static(2 * R_QIDX + 3)
            for m in range(M_GROUP):
                take_low(m)
                if m % 2 == 1:
                    hi_static(2 * R_GROUP + m // 2)
            for h in range(IDX_HEADS):
                act.wait_ge(logits_full, h + 1)
                if h >= RELU:
                    act.wait_ge(score_step, 2 * (h - RELU + 1))
                act.activation(relu[:, h % RELU, :], tp[:, h % 4, 0:KEYS], ACT.Relu,
                               scale=IDX_SCALE).then_inc(relu_done, 1)

            def piece(s):
                g, j = divmod(s, 4)
                m0 = M_GROUP + g * M_PER_GROUP
                if j < 3:
                    for m in {0: (0, 1), 1: (2, 3), 2: (4, 5, 6, 7)}[j]:
                        take_low(m0 + m)
                else:
                    for t in range(TOK):
                        m = m0 + 8 + t
                        act.wait_ge(acc_full, m + 1)
                        act.activation(v_n[:, g % 2, t, 0:S], acc[:, m % 4, 0:S], ACT.Copy)\
                           .then_inc(low_done, 1)

            for s in range(4):
                piece(s)
                hi_static(2 * R_GROUP + 4 + s)
            for s in range(HEADS + 4):
                if s >= 4:
                    act.wait_ge(pv_full, s - 3)
                    act.activation(o_t[:, s - 4, 0, :], tp[:, 3, 0:S], ACT.Copy).then_inc(o_hi, 1)
                if 3 <= s < HEADS + 3:
                    act.wait_ge(pt_full, s - 2)
                    act.activation(prob_t[:, (s - 3) % 2, :], tp[:, 2, 0:KEYS], ACT.Copy).then_inc(pt_done, 1)
                if s < HEADS:
                    for t in range(TOK):
                        act.wait_ge(min_done, 2 * s + t + 1)
                        cols = slice(0, P) if t == 0 else slice(P, KEYS)
                        act.activation(prob[:, s % 3, cols], neg_s[:, s % 2, cols], ACT.Exp, scale=-1.0,
                                       bias=row_min[:, s % 2, t:t + 1],
                                       accum_out=row_sum[:, s % 2, t:t + 1]).then_inc(exp_done, 1)
                if s + 4 < HEADS:
                    piece(s + 4)
                    hi_static(2 * R_GROUP + 8 + s)
                if s == HEADS:
                    hi_static(2 * R_OUT + 4)

            def hi_loop(used, raw_count, half, slot, n=HALF, first=None):
                first = half * n if first is None else first
                if half == 0:
                    act.wait_ge(raw_full[slot], 16 * raw_count)
                act.wait_ge(*used)
                act.activation(w_hi[:, (2 * slot + half) % RING, 0:n], raw[:, slot, first:first + n],
                               ACT.Copy).then_inc(hi_done, 1)

            def take_low_loop(m, bank, c):
                act.wait_ge(acc_full, m + 1)
                act.wait_ge(comb_done, m - 1)
                act.activation(low[:, c, :], acc[:, bank, S:2 * S], ACT.Copy).then_inc(low_done, 1)

            def out_tile(c, i):
                tile = RING * i + c
                for half in (0, 1):
                    hi_loop(used_out(tile - 2, half), R_OUT // RING + 1 + i, half, c)
                take_low_loop(M_OUT + tile - 2, (c - 2) % 4, c % 2)

            hi_loop(used_out(0, 1), R_OUT // RING + 1, 1, 2)
            take_low_loop(M_OUT, 0, 0)
            out_tile(3, 0)
            with act.Fori(1, KD // RING) as i:
                for c in range(RING):
                    out_tile(c, i)
            def hi_first(j):
                if j < 2:
                    act.wait_ge(raw_full[j], 16 * (R_FFN // RING + 1))
                act.wait_ge(*used_out(KD - 2 + j // 2, j % 2))
                act.activation(w_hi[:, j, :], raw[:, j % 2, (j // 2) * HALF:(j // 2 + 1) * HALF],
                               ACT.Copy).then_inc(hi_done, 1)

            hi_first(0)
            hi_first(1)
            take_low_loop(M_OUT + KD - 2, 2, 0)
            hi_first(2)
            take_low_loop(M_OUT + KD - 1, 3, 1)
            load_table(ACT.Sqrt)

            act.wait_ge(var_done, 1)
            act.activation(ln_s, ln_v, ACT.Sqrt).then_inc(sqrt_done, 1)
            act.wait_ge(nmr_done, 1)
            for c in range(ACT_XHAT):
                part = xn[:, 1, c * 512:(c + 1) * 512]
                act.activation(part, part, ACT.Identity, scale=ln_r[:, 1:2], bias=ln_nmr[:, 1:2])\
                   .then_inc(xhat_act, 1)
            for k in range(KD):
                if k == 2:
                    hi_first(3)
                act.wait_ge(xt_full, (k | 1) + 1)
                act.activation(act_t[:, k, 0, :], tp[:, (k // 2) % 4, (k % 2) * S:(k % 2 + 1) * S],
                               ACT.Identity, scale=ln1_gb[:, 0, k:k + 1],
                               bias=ln1_gb[:, 1, k:k + 1]).then_inc(xt_hi, 1)

            def ffn_low_step(tile, c):
                act.wait_ge(ffn_full, tile + 1)
                act.activation(low[:], acc[:, 2 * c:2 * c + 2, S:2 * S], ACT.Copy).then_inc(ffn_low, 1)

            def ffn_silu_step(tile):
                act.wait_ge(ffn_comb, tile + 1)
                act.activation(sig[:], comb[:, 0, :], ACT.Silu).then_inc(ffn_sig, 1)

            def ffn_hi_step(tile):
                act.wait_ge(ffn_hid, tile + 1)
                act.activation(hid_flat[:, bass.ds(tile * 2 * S, S)], hid[:], ACT.Copy).then_inc(ffn_hi, 1)

            def ffn_tile(c, i, older=True):
                tile = 2 * i + c
                for j in range(4):
                    hi_loop(used_ffn(tile - 1, j), R_FFN // RING + 1 + i, j % 2, 2 * c + j // 2)
                    if j == 0 and older:
                        ffn_silu_step(tile - 2)
                    if j == 1 and older:
                        ffn_hi_step(tile - 2)
                ffn_low_step(tile - 1, 1 - c)

            ffn_tile(1, 0, older=False)
            with act.Fori(1, KF // 4) as i:
                ffn_tile(0, i)
                ffn_tile(1, i)
            act.wait_ge(x1_step, 16)
            with act.Fori(KF // 4, KF // 2) as i:
                ffn_tile(0, i)
                ffn_tile(1, i)

            def down_half(j, i):
                used = used_down(i, j - 4) if j >= 4 else \
                    used_ffn(KF - 1, j) if isinstance(i, int) and i == 0 else used_down(i - 1, j + 4)
                hi_loop(used, R_DOWN // RING + 1 + i, j % 2, j // 2,
                        n=DOWN_K[j] * P, first=(j % 2) * DOWN_K[0] * P)

            for j in range(8):
                down_half(j, 0)
                if j == 0:
                    ffn_silu_step(KF - 2)
                if j == 1:
                    ffn_hi_step(KF - 2)
                if j == 3:
                    ffn_low_step(KF - 1, 1)
                    ffn_silu_step(KF - 1)
                    ffn_hi_step(KF - 1)

            def down_tile(c, i):
                for j in range(8):
                    down_half(j, 2 * i + c)
                    if j == 3:
                        take_low_loop(M_DOWN + 2 * i + c - 1, 1 - c, 1 - c)

            down_tile(1, 0)
            with act.Fori(1, KD // 2) as i:
                down_tile(0, i)
                down_tile(1, i)
            take_low_loop(M_DOWN + KD - 1, 1, 1)

            load_table(ACT.Sqrt)
            act.wait_ge(var_done, 2)
            act.activation(ln_s, ln_v, ACT.Sqrt).then_inc(sqrt_done, 1)
            act.wait_ge(nmr_done, 2)
            for c, t in Y_SHARED:
                part = xn[:, t, c * 512:(c + 1) * 512]
                act.activation(part, part, ACT.Identity, scale=ln_r[:, t:t + 1],
                               bias=ln_nmr[:, t:t + 1]).then_inc(y_norm, 1)

        @block.vector
        def _(dve):
            def lo_static(v):
                r, half = divmod(v, 2)
                dve.wait_ge(hi_done, SPLIT_PLACE.get(v, v) + 1)
                if r in X_BLOCKS:
                    k0 = 8 * X_BLOCKS.index(r) + 4 * half
                    src = raw[:, r % RING, half * HALF:(half + 1) * HALF].rearrange("p (k s) -> p k s", s=S)
                    dve.tensor_tensor(act_t[:, k0:k0 + 4, 1, :], src, act_t[:, k0:k0 + 4, 0, :],
                                      ALU.subtract).then_inc(lo_done, 1)
                    return
                w = ring_index(v)
                n = W_IN if r < R_QIDX else HALF
                dve.tensor_tensor(w_lo[:, w % RING, 0:n], raw[:, r % RING, half * n:(half + 1) * n],
                                  w_hi[:, w % RING, 0:n], ALU.subtract).then_inc(lo_done, 1)

            def combine(m, dst):
                dve.wait_ge(low_done, m + 1)
                dve.tensor_tensor(dst, acc[:, m % 4, 0:S], low[:, m % 2, :], ALU.add).then_inc(comb_done, 1)

            for v in SPLIT_ORDER + tuple(range(len(SPLIT_ORDER), 2 * R_QIDX + 2)):
                lo_static(v)

            dve.wait_ge(ssq_done, 4)
            for n, width in enumerate((Q_RANK, KV_RANK)):
                dve.tensor_scalar(rstd4[:, n:4:2], ssq[:, n:4:2], 1.0 / width, EPS, ALU.mult, ALU.add)\
                   .then_inc(rms_var, 1)
            dve.wait_ge(rms_sqrt, 1)
            dve.reciprocal(rms_r, rms_v).then_inc(rms_inv, 1)
            dve.wait_ge(rms_inv, 1)
            dve.tensor_tensor(rms_v, rms_r, rms_r, ALU.mult).then_inc(rms_inv, 1)
            dve.wait_ge(rms_inv, 2)
            dve.scalar_tensor_tensor(out=rms_v, in0=rms_v, scalar=-0.5, in1=rstd4, op0=ALU.mult,
                                     op1=ALU.mult).then_inc(rms_inv, 1)
            dve.wait_ge(rms_inv, 3)
            dve.scalar_tensor_tensor(out=rstd4, in0=rms_v, scalar=1.5, in1=rms_r, op0=ALU.add,
                                     op1=ALU.mult).then_inc(rms_inv, 1)
            dve.wait_ge(rms_inv, 4)
            for t in range(TOK):
                dve.tensor_scalar(proj[:, t, 0:Q_RANK], acc[:, 2 * t, :], rstd4[:, 2 * t:2 * t + 1], None,
                                  ALU.mult).then_inc(proj_q_done, 1)
            for n in range(KQ + KV):
                dve.wait_ge(c_hi, (n | 1) + 1)
                hi_, lo_ = (cq_t[:, n, 0, :], cq_t[:, n, 1, :]) if n < KQ else \
                    (ckv_t[:, n - KQ, 0, :], ckv_t[:, n - KQ, 1, :])
                dve.scalar_tensor_tensor(out=lo_, in0=tp[:, n // 2, (n % 2) * S:(n % 2 + 1) * S],
                                         scalar=rms_g[:, n:n + 1], in1=hi_, op0=ALU.mult,
                                         op1=ALU.subtract).then_inc(c_lo, 1)
            lo_static(2 * R_QIDX + 2)
            lo_static(2 * R_QIDX + 3)
            for m in range(M_GROUP):
                combine(m, qidx_t[:, m, :])
                if m % 2 == 1:
                    lo_static(2 * R_GROUP + m // 2)

            w0 = Q_RANK + KV_RANK + 2 * IDX_DIM
            blocks = ((0, slice(0, P)), (1, slice(P, KEYS)))
            for h in range(IDX_HEADS):
                dve.wait_ge(relu_done, h + 1)
                for t, cols in blocks:
                    w_idx = proj[:, t, w0 + h:w0 + h + 1]
                    if h == 0:
                        dve.tensor_scalar(score[:, cols], relu[:, 0, cols], w_idx, None, ALU.mult)\
                           .then_inc(score_step, 1)
                    else:
                        dve.wait_ge(score_step, 2 * (h - 1) + t + 1)
                        dve.scalar_tensor_tensor(out=score[:, cols], in0=relu[:, h % RELU, cols], scalar=w_idx,
                                                 in1=score[:, cols], op0=ALU.mult, op1=ALU.add)\
                           .then_inc(score_step, 1)

            def piece(s):
                g, j = divmod(s, 4)
                m0 = M_GROUP + g * M_PER_GROUP
                if j < 2:
                    for n in range(2):
                        combine(m0 + 2 * j + n, q_t[:, g % 2, 2 * j + n, :])
                elif j == 2:
                    for n in range(GH):
                        combine(m0 + GH + n, k_t[:, g % 2, n, :])
                else:
                    for t in range(TOK):
                        m = m0 + 2 * GH + t
                        dve.wait_ge(low_done, m + 1)
                        dve.tensor_copy(v_n[:, g % 2, t, S:2 * S], acc[:, m % 4, S:2 * S]).then_inc(comb_done, 1)

            dve.wait_ge(score_masked, 2)
            for n in range(TOPK // 8):
                src = score if n == 0 else work
                if n > 0:
                    dve.wait_ge(top_step, 4 * n)
                for t, cols in blocks:
                    dve.max(top8[:, t, :], src[:, cols]).then_inc(top_step, 1)
                for t, cols in blocks:
                    dve.wait_ge(top_step, 4 * n + t + 1)
                    dve.match_replace(work[:, cols], top8[:, t, :], src[:, cols], TAKEN).then_inc(top_step, 1)
                if n % 2 == 0:
                    piece(n // 2)
            dve.wait_ge(top_step, 4 * (TOPK // 8))
            dve.tensor_scalar(key_bias[:], work[:], NOT_TAKEN, MASKED, ALU.is_gt, ALU.mult).then_inc(bias_raw, 1)
            dve.wait_ge(bias_done, 2)

            for s in range(HEADS + 4):
                if s >= 4:
                    dve.wait_ge(o_hi, s - 3)
                    dve.tensor_tensor(o_t[:, s - 4, 1, :], tp[:, 3, 0:S], o_t[:, s - 4, 0, :],
                                      ALU.subtract).then_inc(o_lo, 1)
                if s < HEADS:
                    dve.wait_ge(qk_full, s + 1)
                    dve.scalar_tensor_tensor(out=neg_s[:, s % 2, :], in0=tp[:, s % 2, 0:KEYS],
                                             scalar=-ATTN_SCALE, in1=key_bias[:], op0=ALU.mult,
                                             op1=ALU.add).then_inc(neg_done, 1)
                    if s >= 1:
                        dve.wait_ge(exp_done, 2 * s)
                        if s >= 3:
                            dve.wait_ge(prob_done, 2 * (s - 2))
                        dve.reciprocal(row_inv[:, s % 2, :], row_sum[:, (s - 1) % 2, :]).then_inc(inv_done, 1)
                    dve.wait_ge(neg_done, s + 1)
                    for t, cols in blocks:
                        dve.tensor_reduce(row_min[:, s % 2, t:t + 1], neg_s[:, s % 2, cols], AX.X, ALU.min)\
                           .then_inc(min_done, 1)
                if s == HEADS:
                    dve.wait_ge(exp_done, 2 * s)
                    dve.wait_ge(prob_done, 2 * (s - 2))
                    dve.reciprocal(row_inv[:, s % 2, :], row_sum[:, (s - 1) % 2, :]).then_inc(inv_done, 1)
                if 1 <= s <= HEADS - 4:
                    if s == 1:
                        dve.wait_ge(lo_done, 2 * R_GROUP + 8)
                    lo_static(2 * R_GROUP + 7 + s)
                if POOL_NORM < s <= HEADS:
                    dve.wait_ge(inv_done, s)
                    dve.wait_ge(prob_done, 2 * (s - 1))
                    for t, cols in blocks:
                        dve.tensor_scalar(prob[:, (s - 1) % 3, cols], prob[:, (s - 1) % 3, cols],
                                          row_inv[:, s % 2, t:t + 1], None, ALU.mult).then_inc(prob_done, 1)
                if s + 4 < HEADS:
                    piece(s + 4)
                if s == HEADS:
                    lo_static(2 * R_OUT + 4)

            def lo_loop(v, half, slot, n=HALF, first=None):
                first = half * n if first is None else first
                dve.wait_ge(hi_done, v + 1)
                h = (2 * slot + half) % RING
                dve.tensor_tensor(w_lo[:, h, 0:n], raw[:, slot, first:first + n], w_hi[:, h, 0:n],
                                  ALU.subtract).then_inc(lo_done, 1)

            def combine_loop(m, bank, c):
                dve.wait_ge(low_done, m + 1)
                dve.tensor_tensor(comb[:, c % 2, :], acc[:, bank, 0:S], low[:, c % 2, :], ALU.add)\
                   .then_inc(comb_done, 1)

            def residual(n, bank, tile):
                col = bass.ds(tile * P, P)
                dve.wait_ge(m_tp, n + 1)
                dve.scalar_tensor_tensor(out=xn[:, :, col], in0=xn[:, :, col], scalar=ALPHA,
                                         in1=tp[:, bank, 0:S].rearrange("p (t s) -> p t s", t=TOK),
                                         op0=ALU.mult, op1=ALU.add).then_inc(res_done, 1)
                dve.wait_ge(res_done, n + 1)
                for t in range(TOK):
                    dve.bn_stats(stats[:, t, bass.ds(tile * 6, 6)], xn[:, t, col]).then_inc(stat_done, 1)

            dve.wait_ge(xn_full, 16)

            def out_tile(c, i):
                tile = RING * i + c
                for half in (0, 1):
                    lo_loop(2 * R_OUT + 2 * tile + half, half, c)
                combine_loop(M_OUT + tile - 2, (c - 2) % 4, c)
                residual(tile - 3, (c - 3) % 4, tile - 3)

            lo_loop(2 * R_OUT + 5, 1, 2)
            combine_loop(M_OUT, 0, 0)
            out_tile(3, 0)
            with dve.Fori(1, KD // RING) as i:
                for c in range(RING):
                    out_tile(c, i)
            def lo_first(j):
                dve.wait_ge(hi_done, 2 * R_FFN + j + 1)
                dve.tensor_tensor(w_lo[:, j, :], raw[:, j % 2, (j // 2) * HALF:(j // 2 + 1) * HALF],
                                  w_hi[:, j, :], ALU.subtract).then_inc(lo_done, 1)

            lo_first(0)
            residual(KD - 3, (KD - 3) % 4, KD - 3)
            lo_first(1)
            combine_loop(M_OUT + KD - 2, 2, 0)
            lo_first(2)
            combine_loop(M_OUT + KD - 1, 3, 1)
            residual(KD - 2, (KD - 2) % 4, KD - 2)
            residual(KD - 1, (KD - 1) % 4, KD - 1)

            def row_stats(which):
                dve.wait_ge(stat_done, TOK * KD * which)
                for t in range(TOK):
                    dve.bn_aggr(mean_var[:, 2 * t:2 * t + 2], stats[:, t, :])\
                       .then_inc(aggr_done, 1)
                dve.wait_ge(aggr_done, TOK * which)
                dve.tensor_scalar(ln_v, mean_var[:, 1:4:2], EPS, None, ALU.add).then_inc(var_done, 1)
                dve.wait_ge(sqrt_done, which)
                dve.reciprocal(ln_r, ln_s).then_inc(rstd_done, 1)
                dve.wait_ge(rstd_done, which)

            def shift():
                dve.scalar_tensor_tensor(out=ln_nmr, in0=mean_var[:, 0:4:2], scalar=-1.0, in1=ln_r,
                                         op0=ALU.mult, op1=ALU.mult).then_inc(nmr_done, 1)

            row_stats(1)
            shift()
            for c in range(4):
                for t in range(1 if c < ACT_XHAT else TOK):
                    part = xn[:, t, c * 512:(c + 1) * 512]
                    dve.tensor_scalar(part, part, mean_var[:, 2 * t:2 * t + 1], ln_r[:, t:t + 1],
                                      ALU.subtract, ALU.mult).then_inc(xhat_done, 1)
            vals = (low, comb)

            def value(k):
                dve.wait_ge(xt_hi, (k | 1) + 1)
                if k - 4 in POOL_LO:
                    dve.wait_ge(xt_lo_pool, len([u for u in POOL_LO if u <= k - 4]))
                dve.tensor_scalar(vals[(k // 2) % 2][:, k % 2, :],
                                  tp[:, (k // 2) % 4, (k % 2) * S:(k % 2 + 1) * S],
                                  ln1_gb[:, 0, k:k + 1], ln1_gb[:, 1, k:k + 1], ALU.mult, ALU.add)\
                    .then_inc(xt_val, 1)

            def value_lo(k):
                if k not in POOL_LO:
                    dve.wait_ge(xt_val, k + 1)
                    dve.tensor_tensor(act_t[:, k, 1, :], vals[(k // 2) % 2][:, k % 2, :], act_t[:, k, 0, :],
                                      ALU.subtract).then_inc(xt_lo, 1)

            for k in range(0, KD, 2):
                value(k)
                value(k + 1)
                value_lo(k)
                value_lo(k + 1)
            dve.wait_ge(lo_done, 2 * R_FFN + 4)

            def ffn_combine(tile, c):
                dve.wait_ge(ffn_low, tile + 1)
                dve.tensor_tensor(comb[:], acc[:, 2 * c:2 * c + 2, 0:S], low[:], ALU.add).then_inc(ffn_comb, 1)

            def ffn_mul(tile):
                dve.wait_ge(ffn_sig, tile + 1)
                dve.tensor_tensor(hid[:], sig[:], comb[:, 1, :], ALU.mult).then_inc(ffn_hid, 1)

            def ffn_lo_step(tile):
                dve.wait_ge(ffn_hi, tile + 1)
                dve.tensor_tensor(hid_flat[:, bass.ds(tile * 2 * S + S, S)], hid[:],
                                  hid_flat[:, bass.ds(tile * 2 * S, S)], ALU.subtract).then_inc(ffn_lo, 1)

            def ffn_tile(c, i, older=True):
                tile = 2 * i + c
                for j in range(4):
                    lo_loop(2 * R_FFN + 4 * tile + j, j % 2, 2 * c + j // 2)
                    if j == 0 and older:
                        ffn_mul(tile - 2)
                    if j == 1 and older:
                        ffn_lo_step(tile - 2)
                ffn_combine(tile - 1, 1 - c)

            ffn_tile(1, 0, older=False)
            with dve.Fori(1, KF // 4) as i:
                ffn_tile(0, i)
                ffn_tile(1, i)
            dve.wait_ge(x1_step, 16)
            with dve.Fori(KF // 4, KF // 2) as i:
                ffn_tile(0, i)
                ffn_tile(1, i)

            def down_half(j, i):
                lo_loop(2 * R_DOWN + 8 * i + j, j % 2, j // 2, n=DOWN_K[j] * P, first=(j % 2) * DOWN_K[0] * P)

            for j in range(8):
                down_half(j, 0)
                if j == 0:
                    ffn_mul(KF - 2)
                if j == 1:
                    ffn_lo_step(KF - 2)
                if j == 3:
                    ffn_combine(KF - 1, 1)
                    ffn_mul(KF - 1)
                    ffn_lo_step(KF - 1)

            def down_tile(c, i):
                prev = 2 * i + c - 1
                for j in range(8):
                    down_half(j, 2 * i + c)
                    if j == 3:
                        combine_loop(M_DOWN + prev, 1 - c, 1 - c)
                    if j == 6:
                        residual(KD + prev, 1 - c, prev)

            down_tile(1, 0)
            with dve.Fori(1, KD // 2) as i:
                down_tile(0, i)
                down_tile(1, i)
            combine_loop(M_DOWN + KD - 1, 1, 1)
            residual(2 * KD - 1, 1, KD - 1)

            row_stats(2)
            shift()
            dve.wait_ge(ln2_rows_full, 32)
            def y_own(n):
                c, t = Y_OWN[n]
                part = xn[:, t, c * 512:(c + 1) * 512]
                dve.scalar_tensor_tensor(out=part, in0=part, scalar=mean_var[:, 2 * t:2 * t + 1],
                                         in1=ln2_rows[:, 0, c * 512:(c + 1) * 512], op0=ALU.subtract,
                                         op1=ALU.mult).then_inc(y_scaled, 1)
                dve.wait_ge(y_scaled, n + 1)
                dve.scalar_tensor_tensor(out=part, in0=part, scalar=ln_r[:, t:t + 1],
                                         in1=ln2_rows[:, 1, c * 512:(c + 1) * 512], op0=ALU.mult,
                                         op1=ALU.add).then_inc(y_own_done, 1)

            def y_shared(n):
                c, t = Y_SHARED[n]
                part = xn[:, t, c * 512:(c + 1) * 512]
                dve.wait_ge(y_norm, n + 1)
                dve.tensor_tensor(part, part, ln2_rows[:, 0, c * 512:(c + 1) * 512], ALU.mult)\
                   .then_inc(y_gain, 1)

            for own, n in Y_ORDER:
                (y_own if own else y_shared)(n)

        @block.gpsimd
        def _(pool):
            pool.dma_start(rms_g[:], a["rms_g_t"]).then_inc(rms_full, 16)
            pool.memset(table_in[:], 1.0).then_inc(table_set, 1)
            pool.memset(ident[:], 0.0).then_inc(ident_done, 1)
            pool.wait_ge(ident_done, 1)
            pool.affine_select(out=ident[:], in_=ident[:], compare_op=ALU.not_equal, fill=1.0, base=0,
                               pattern=[[-1, P]], channel_multiplier=1).then_inc(ident_done, 1)
            blocks = ((0, slice(0, P), P), (1, slice(P, KEYS), S))
            pool.wait_ge(score_step, 2 * IDX_HEADS)
            for t, cols, n in blocks:
                pool.affine_select(out=score[:, cols], in_=score[:, cols], compare_op=ALU.is_ge,
                                   fill=NOT_CAUSAL, base=t * P, pattern=[[-1, n]], channel_multiplier=1)\
                    .then_inc(score_masked, 1)
            def lo_pool(v):
                pool.wait_ge(hi_done, v + 1)
                pool.wait_ge(lo_done, v)
                w = ring_index(v) % RING
                pool.tensor_tensor(w_lo[:, w, :], raw[:, v // 2 % RING, v % 2 * HALF:(v % 2 + 1) * HALF],
                                   w_hi[:, w, :], ALU.subtract).then_inc(lo_done, 1)

            for v in range(2 * R_GROUP + 4, 2 * R_GROUP + 7):
                lo_pool(v)
            pool.wait_ge(bias_raw, 1)
            for t, cols, n in blocks:
                pool.affine_select(out=key_bias[:, cols], in_=key_bias[:, cols], compare_op=ALU.is_ge,
                                   fill=MASKED, base=t * P, pattern=[[-1, n]], channel_multiplier=1)\
                    .then_inc(bias_done, 1)
            lo_pool(2 * R_GROUP + 7)
            for s in range(POOL_NORM):
                pool.wait_ge(inv_done, s + 1)
                for t, cols, n in blocks:
                    pool.tensor_scalar(prob[:, s % 3, cols], prob[:, s % 3, cols],
                                       row_inv[:, (s + 1) % 2, t:t + 1], None, ALU.mult).then_inc(prob_done, 1)
            vals = (low, comb)
            for k in POOL_LO:
                if k == POOL_LO[1]:
                    pool.wait_ge(hi_done, 2 * R_FFN + 4)
                    pool.wait_ge(lo_done, 2 * R_FFN + 3)
                    pool.tensor_tensor(w_lo[:, 3, :], raw[:, 1, HALF:RAW_ELEMS], w_hi[:, 3, :],
                                       ALU.subtract).then_inc(lo_done, 1)
                pool.wait_ge(xt_hi, k + 1)
                pool.wait_ge(xt_val, k + 1)
                pool.tensor_tensor(act_t[:, k, 1, :], vals[(k // 2) % 2][:, k % 2, :], act_t[:, k, 0, :],
                                   ALU.subtract).then_inc(xt_lo_pool, 1)
            pool.wait_ge(ln1_rows_full, 32)
            pool.wait_ge(xt_full, KD)
            n = 0
            for c in range(4):
                for t in range(TOK):
                    part = xn[:, t, c * 512:(c + 1) * 512]
                    pool.tensor_tensor(part, part, ln1_rows[:, 0, c * 512:(c + 1) * 512], ALU.mult)\
                        .then_inc(x1_step, 1)
                    n += 1
                    pool.wait_ge(x1_step, n)
                    pool.tensor_tensor(part, part, ln1_rows[:, 1, c * 512:(c + 1) * 512], ALU.add)\
                        .then_inc(x1_step, 1)
                    n += 1
            pool.wait_ge(ln2_rows_full, 32)
            for n, (c, t) in enumerate(Y_SHARED):
                part = xn[:, t, c * 512:(c + 1) * 512]
                pool.wait_ge(y_gain, n + 1)
                pool.tensor_tensor(part, part, ln2_rows[:, 1, c * 512:(c + 1) * 512], ALU.add)\
                    .then_inc(y_done, 1)

        @block.tensor
        def _(pe):
            def pair(bank, w, e0, rhs, start, stop):
                wh = w_hi[:, w, e0:e0 + P]
                wl = w_lo[:, w, e0:e0 + P]
                if start:
                    pe.matmul(acc[:, bank, :], wh, rhs, start=True, stop=False)
                    return pe.matmul(acc[:, bank, 0:S], wl, rhs[:, 0, :], start=False, stop=False,
                                     skip_group_check=True)
                pe.matmul(acc[:, bank, 0:S], wl, rhs[:, 0, :], start=False, stop=False, skip_group_check=True)
                return pe.matmul(acc[:, bank, :], wh, rhs, start=False, stop=stop)

            spans = ((0, 0, Q_RANK), (1, Q_RANK, W_IN))
            for k in range(KD):
                v = 2 * IN_BLOCKS[k // 2] + k % 2
                w = ring_index(v) % RING
                pe.wait_ge(lo_done, SPLIT_PLACE.get(v, v) + 1)
                if k == 4:
                    pe.wait_ge(lo_done, len(SPLIT_ORDER))
                for t in range(TOK):
                    for x_part, w_part in ((0, w_hi), (0, w_lo), (1, w_hi)):
                        for b, c0, c1 in spans:
                            last = pe.matmul(acc[:, 2 * t + b, 0:c1 - c0],
                                             act_t[:, k, x_part, t * P:(t + 1) * P], w_part[:, w, c0:c1],
                                             start=(k == 0 and x_part == 0 and w_part is w_hi),
                                             stop=(k == KD - 1 and x_part == 1))
                last.then_inc(pe_used, 1)
            pe.wait_ge(ident_done, 2)
            for t in range(TOK):
                for n in range(KQ + KV + 1):
                    if n == 0:
                        pe.wait_ge(proj_q_done, t + 1)
                    if n == KQ:
                        pe.wait_ge(proj_done, 2 * TOK + t + 1)
                    last = pe.transpose(tp[:, n // 2, (n % 2) * S + t * P:(n % 2) * S + (t + 1) * P],
                                        proj[:, t, n * P:(n + 1) * P], ident[:])
                    if t == TOK - 1:
                        last.then_inc(proj_t, 1)

            def project(v, tiles, kts, act_tiles, m0):
                w = ring_index(v) % RING
                pe.wait_ge(lo_done, v + 1)
                for n in range(tiles):
                    m = m0 + n
                    if m >= 4:
                        pe.wait_ge(comb_done, m - 3)
                    for k in range(kts):
                        last = pair(m % 4, w, (n * kts + k) * P, act_tiles[:, k, :, :], k == 0, k == kts - 1)
                    last.then_inc(acc_full, 1)

            pe.wait_ge(proj_done, 3 * TOK)
            pe.wait_ge(c_lo, KQ)
            for half in range(4):
                project(2 * R_QIDX + half, 2, KQ, cq_t, M_QIDX + 2 * half)

            pe.wait_ge(c_hi, KQ + KV + 1)
            pe.wait_ge(c_lo, KQ + KV)
            for h in range(IDX_HEADS):
                pe.wait_ge(comb_done, h // 2 + 1)
                if h >= 4:
                    pe.wait_ge(relu_done, h - 3)
                rows = slice(IDX_DIM * (h % 2), IDX_DIM * (h % 2) + IDX_DIM)
                for t, c0, n in ((0, 0, P), (1, P, S)):
                    last = pe.matmul(tp[:, h % 4, c0:c0 + n], qidx_t[rows, h // 2, t * P:(t + 1) * P],
                                     kidx_t[rows, 0:n], start=True, stop=True)
                last.then_inc(logits_full, 1)

            def piece(s):
                g, j = divmod(s, 4)
                m0 = M_GROUP + g * M_PER_GROUP
                v = 2 * R_GROUP + s
                if j < 2:
                    project(v, 2, KQ, cq_t, m0 + 2 * j)
                elif j == 2:
                    project(v, GH, KV, ckv_t, m0 + GH)
                else:
                    w = ring_index(v) % RING
                    pe.wait_ge(lo_done, v + 1)
                    for t in range(TOK):
                        m = m0 + 2 * GH + t
                        pe.wait_ge(comb_done, m - 3)
                        steps = [(k, x, wp) for k in range(KV) for x, wp in ((0, w_hi), (0, w_lo), (1, w_hi))]
                        for n, (k, x, wp) in enumerate(steps):
                            last = pe.matmul(acc[:, m % 4, :], ckv_t[:, k, x, t * P:(t + 1) * P],
                                             wp[:, w, k * 512:(k + 1) * 512], start=(n == 0),
                                             stop=(n == len(steps) - 1))
                        last.then_inc(acc_full, 1)

            for s in range(4):
                piece(s)
            pe.wait_ge(relu_done, IDX_HEADS)
            def out_part(tile, k0, k1):
                if k0 == 0:
                    pe.wait_ge(comb_done, M_OUT + tile - 3)
                for k in range(k0, k1):
                    half = k // 8
                    if k % 8 == 0:
                        pe.wait_ge(lo_done, 2 * R_OUT + 2 * tile + half + 1)
                    pe.wait_ge(o_lo, k + 1)
                    last = pair(tile, 2 * tile + half, (k % 8) * P, o_t[:, k, :, :], k == 0, k == KD - 1)
                    if k % 8 == 7:
                        last.then_inc(*((pe_used, 1) if half == 0 else (acc_full, 1)))

            out_parts = {12: ((0, 0, 4),), 13: ((0, 4, 8),), 14: ((1, 0, 4),), 15: ((1, 4, 8),),
                         16: ((0, 8, 11),), 17: ((0, 11, 12), (1, 8, 11)),
                         18: ((1, 11, 12), (0, 12, 14), (1, 12, 14))}
            for s in range(HEADS + 3):
                if s < HEADS:
                    g, h = divmod(s, GH)
                    pe.wait_ge(comb_done, M_GROUP + g * M_PER_GROUP + 2 * GH)
                    if s >= 2:
                        pe.wait_ge(neg_done, s - 1)
                    for t, c0, n in ((0, 0, P), (1, P, S)):
                        last = pe.matmul(tp[:, s % 2, c0:c0 + n], q_t[:, g % 2, h, t * P:(t + 1) * P],
                                         k_t[:, g % 2, h, 0:n], start=True, stop=True)
                    last.then_inc(qk_full, 1)
                if s + 4 < HEADS:
                    piece(s + 4)
                for part in out_parts.get(s, ()):
                    out_part(*part)
                if 2 <= s < HEADS + 2:
                    u = s - 2
                    pe.wait_ge(prob_done, 2 * u + 2)
                    if u >= 1:
                        pe.wait_ge(pt_done, u)
                    for n in range(KEYS // P):
                        last = pe.transpose(tp[:, 2, n * P:(n + 1) * P], prob[:, u % 3, n * P:(n + 1) * P],
                                            ident[:])
                    last.then_inc(pt_full, 1)
                if s >= 3:
                    u = s - 3
                    g, h = divmod(u, GH)
                    pe.wait_ge(pt_done, u + 1)
                    if u >= 1:
                        pe.wait_ge(o_lo, u)
                    pe.wait_ge(comb_done, M_GROUP + (g + 1) * M_PER_GROUP)
                    v_h = [v_n[:, g % 2, t, h * HD:(h + 1) * HD] for t in range(TOK)]
                    pe.matmul(tp[:, 3, 0:P], v_h[0], prob_t[:, u % 2, 0:P], start=True, stop=True)
                    pe.matmul(tp[:, 3, P:S], v_h[0], prob_t[:, u % 2, P:2 * P], start=True, stop=False)
                    pe.matmul(tp[:, 3, P:S], v_h[1], prob_t[:, u % 2, 2 * P:3 * P], start=False,
                              stop=True).then_inc(pv_full, 1)

            def turn(n, bank, c):
                for t in range(TOK):
                    last = pe.transpose(tp[:, bank, t * P:(t + 1) * P], comb[:, c, t * P:(t + 1) * P], ident[:])
                last.then_inc(m_tp, 1)

            out_part(0, 14, KD)
            out_part(1, 14, KD)
            def turn_out(tile, c, i):
                pe.wait_ge(comb_done, M_OUT + tile)
                if not (isinstance(i, int) and tile <= 4):
                    pe.wait_ge(res_done, tile - 4)
                turn(tile - 1, (c - 1) % 4, (c - 1) % 2)

            def out_tile(c, i, between=None):
                tile = RING * i + c
                pe.wait_ge(comb_done, M_OUT + tile - 3)
                for half in (0, 1):
                    if half == 1 and between:
                        between()
                    pe.wait_ge(lo_done, 2 * R_OUT + 2 * tile + half + 1)
                    for n in range(8):
                        k = 8 * half + n
                        last = pair(c, (2 * c + half) % RING, n * P, o_t[:, k, :, :], k == 0, k == KD - 1)
                    last.then_inc(*((pe_used, 1) if half == 0 else (acc_full, 1)))
                turn_out(tile, c, i)

            out_tile(2, 0, between=lambda: turn_out(1, 1, 0))
            for tile in range(3, 2 * RING):
                out_tile(tile % RING, tile // RING)
            with pe.Fori(2, KD // RING) as i:
                for c in range(RING):
                    out_tile(c, i)
            pe.wait_ge(comb_done, M_OUT + KD)
            turn(KD - 1, 3, 1)

            def turn_in(k):
                if k % 4 == 0:
                    c = k // 4
                    pe.wait_ge(xhat_done, c + 1 + max(0, c + 1 - ACT_XHAT))
                    pe.wait_ge(xhat_act, min(c + 1, ACT_XHAT))
                if k % 2 == 0 and k >= 8:
                    pe.wait_ge(xt_hi, k - 6)
                    pe.wait_ge(xt_val, k - 6)
                for t in range(TOK):
                    c0 = (k % 2) * S + t * P
                    last = pe.transpose(tp[:, (k // 2) % 4, c0:c0 + P], xn[:, t, k * P:(k + 1) * P], ident[:])
                last.then_inc(xt_full, 1)

            for k in range(8):
                turn_in(k)

            def first_tile():
                for n in range(2):
                    for j in (2 * n, 2 * n + 1):
                        pe.wait_ge(lo_done, 2 * R_FFN + j + 1)
                    for k in range(8 * n, 8 * n + 8):
                        pe.wait_ge(xt_lo, len([u for u in range(k + 1) if u not in POOL_LO]))
                        if k in POOL_LO:
                            pe.wait_ge(xt_lo_pool, len([u for u in POOL_LO if u <= k]))
                        for j in (2 * n, 2 * n + 1):
                            last = pair(j % 2, j, (k % 8) * P, act_t[:, k, :, :], k == 0, k == KD - 1)
                            if k % 8 == 7:
                                last.then_inc(*((pe_used, 1) if j < 3 else (ffn_full, 1)))
                        if k % 2 == 1 and k < 8:
                            turn_in(k + 7)
                            turn_in(k + 8)

            def ffn_tile(c, i):
                tile = 2 * i + c
                if not (isinstance(i, int) and i == 0):
                    pe.wait_ge(ffn_comb, tile - 1)
                for j in range(4):
                    pe.wait_ge(lo_done, 2 * R_FFN + 4 * tile + j + 1)
                    for n in range(8):
                        k = 8 * (j % 2) + n
                        last = pair(2 * c + j // 2, j, n * P, act_t[:, k, :, :], k == 0, k == KD - 1)
                    last.then_inc(*((pe_used, 1) if j < 3 else (ffn_full, 1)))

            first_tile()
            ffn_tile(1, 0)
            with pe.Fori(1, KF // 2) as i:
                ffn_tile(0, i)
                ffn_tile(1, i)

            def down_tile(c, i, first=False, second=False):
                tile = 2 * i + c
                if first:
                    pe.wait_ge(ffn_comb, KF - 1)
                elif second:
                    pe.wait_ge(ffn_comb, KF)
                else:
                    pe.wait_ge(comb_done, M_DOWN + tile - 1)
                k = 0
                for j in range(8):
                    pe.wait_ge(lo_done, 2 * R_DOWN + 8 * tile + j + 1)
                    if first and j in (0, 7):
                        pe.wait_ge(ffn_lo, KF if j == 7 else KF - 2)
                    for n in range(DOWN_K[j]):
                        last = pair(c, j % RING, n * P, hid_t[:, k, :, :], k == 0, k == KF - 1)
                        k += 1
                    last.then_inc(*((pe_used, 1) if j < 7 else (acc_full, 1)))
                    if j == 2 and not first:
                        pe.wait_ge(comb_done, M_DOWN + tile)
                        if not second:
                            pe.wait_ge(res_done, KD + tile - 2)
                        turn(KD + tile - 1, 1 - c, 1 - c)

            down_tile(0, 0, first=True)
            down_tile(1, 0, second=True)
            with pe.Fori(1, KD // 2) as i:
                down_tile(0, i)
                down_tile(1, i)
            pe.wait_ge(comb_done, M_DOWN + KD)
            turn(2 * KD - 1, 1, 1)


_OUT = ((1, S, D), "float32")


def kernel(**inputs):
    from concourse import bacc
    from concourse.bass_utils import run_bass_kernel_spmd

    w = {n: np.asarray(v) for n, v in inputs.items()}

    def k_tiles(m, cols):
        k, n = m.shape
        return m.reshape(k // P, P, n // cols, cols).transpose(2, 1, 0, 3).reshape(n // cols, P, -1)

    x = w["x"].reshape(S, D)
    uq = k_tiles(w["l0_w_uq"], P).reshape(GROUPS, GH, P, -1).transpose(0, 2, 1, 3).reshape(GROUPS, P, -1)
    uk = w["l0_w_uk"].reshape(GROUPS, GH, HD, KV, P).transpose(0, 4, 1, 3, 2).reshape(GROUPS, P, -1)
    uv = w["l0_w_uv"].reshape(GROUPS, GH, KV, P, HD).transpose(0, 3, 2, 1, 4).reshape(GROUPS, P, -1)
    gate, up = (k_tiles(w[n], P) for n in ("l0_ffn_gate", "l0_ffn_up"))
    down = k_tiles(w["l0_ffn_down"], P).reshape(KD, P, 4, 11 * P).transpose(0, 2, 1, 3)
    arrays = {
        "x": x,
        "x_t": x.T.reshape(2, 8, P, S).transpose(0, 2, 1, 3).reshape(2, P, -1),
        "w_in": w["l0_w_in"].reshape(8, 2, P, W_IN).transpose(0, 2, 1, 3).reshape(8, P, -1),
        "w_qidx": k_tiles(w["l0_w_qidx"], P).reshape(2, 4, P, -1).transpose(0, 2, 1, 3).reshape(2, P, -1),
        "w_uq": uq,
        "w_ukv": np.concatenate([uk, uv], axis=2),
        "w_out": k_tiles(w["l0_w_out"], P),
        "w_gu": np.stack([gate, up], axis=1).reshape(2 * KF, P, -1),
        "w_down": down.reshape(4 * KD, P, -1),
        "rms_g_t": np.concatenate([w["l0_q_norm"].reshape(KQ, P), w["l0_kv_norm"].reshape(KV, P)]).T,
        "ln1_gb_t": np.stack([w["l0_ln1_g"], w["l0_ln1_b"]]).reshape(2, KD, P).transpose(2, 0, 1),
        "ln_rows": np.stack([w["l0_ln1_g"], w["l0_ln1_b"], w["l0_ln2_g"], w["l0_ln2_b"]]),
    }
    nc = bacc.Bacc("TRN2", target_bir_lowering=False, num_devices=1)
    feed, aps = {}, {}
    for name, value in arrays.items():
        value = np.ascontiguousarray(value)
        feed["in_" + name] = value
        aps[name] = nc.dram_tensor("in_" + name, value.shape, mybir.dt.from_np(value.dtype),
                                   kind="ExternalInput").ap()
    aps["out"] = nc.dram_tensor("out_0", (S, D), F32, kind="ExternalOutput").ap()
    layer_kernel(nc, aps)
    r = run_bass_kernel_spmd(nc, [feed], core_ids=[0])
    return r.results[0]["out_0"].reshape(_OUT[0])
```

```python
from contextlib import ExitStack

import numpy as np

import concourse.bass as bass
from concourse import mybir

F32 = mybir.dt.float32
F32R = mybir.dt.float32r
ACT = mybir.ActivationFunctionType
ALU = mybir.AluOpType
AX = mybir.AxisListType

P = 128
D = 2048
S = 256
TOK = S // P
KD = D // P
Q_RANK = 512
KV_RANK = 256
IDX_DIM = 64
IDX_HEADS = 16
HEADS = 16
HD = 128
TOPK = min(256, S // 4)
FFN = 5632
KF = FFN // P
ALPHA = 2.0 ** 0.25
EPS = 1e-5
ATTN_SCALE = HD ** -0.5
IDX_SCALE = (IDX_HEADS ** -0.5) * (IDX_DIM ** -0.5)
W_IN = Q_RANK + KV_RANK + IDX_DIM + IDX_HEADS
KQ = Q_RANK // P
KV = KV_RANK // P
GH = 4
GROUPS = HEADS // GH
KEYS = S + P
MASKED = 1e30
NOT_CAUSAL = -3.0e38
TAKEN = -3.4e38
NOT_TAKEN = -3.2e38

RAW_ELEMS = 2048
HALF = RAW_ELEMS // 2
RING = 4
X_BLOCKS = (0, 2)
IN_BLOCKS = (1, 3, 4, 5, 6, 7, 8, 9)
R_QIDX = 10
R_GROUP = 12
R_OUT = R_GROUP + 2 * GROUPS
R_FFN = R_OUT + KD
R_DOWN = R_FFN + 2 * KF
POOL_LO = (1, 5, 9, 13)
POOL_NORM = HEADS - GH
PIECE_AT = (0, 2, 4, 5)
RELU = 3
Y_SHARED = ((0, 0), (0, 1), (1, 0), (2, 0), (3, 0))
Y_OWN = ((1, 1), (2, 1), (3, 1))
Y_ORDER = ((1, 0), (0, 0), (0, 1), (1, 1), (0, 2), (0, 3), (0, 4), (1, 2))
ACT_XHAT = 3
GC = 512
COL_GROUPS = D // GC
OUT_K = HALF // GC
OUT_HALVES = KD // OUT_K
DOWN_K = (2, 1) * 4 + (2, 2) * 8
DOWN_BLOCKS = len(DOWN_K) // 2
DOWN_K0 = tuple(sum(DOWN_K[:h]) for h in range(len(DOWN_K)))

M_QIDX = 0
M_GROUP = M_QIDX + IDX_HEADS * IDX_DIM // P
M_PER_GROUP = 2 * GH + TOK
M_OUT = M_GROUP + GROUPS * M_PER_GROUP
M_DOWN = M_OUT + COL_GROUPS

USED_FFN = KD + (OUT_HALVES - 1) * COL_GROUPS
USED_DOWN = USED_FFN + 3 * KF


SPLIT_ORDER = (0, 2, 3, 1)
SPLIT_PLACE = {v: n for n, v in enumerate(SPLIT_ORDER)}


def ring_index(v):
    x_before = sum(1 for b in X_BLOCKS for h in (0, 1) if 2 * b + h < v)
    return v - x_before


def layer_kernel(nc, a):
    ctx = ExitStack()
    with ctx:
        def sb(name, shape, dt=F32):
            return ctx.enter_context(nc.sbuf_tensor(name, shape, dt))

        def sem(name):
            return ctx.enter_context(nc.semaphore(name))

        raw = sb("raw", [P, RING, RAW_ELEMS])
        w_hi = sb("w_hi", [P, RING, HALF], F32R)
        w_lo = sb("w_lo", [P, RING, HALF], F32R)
        base_a = nc.sbuf_base
        act_t = sb("act_t", [P, KD, 2, S], F32R)
        base_r = nc.sbuf_base
        hid_t = sb("hid_t", [P, KF, 2, S], F32R)
        xn = sb("xn", [P, TOK, D])
        ident = sb("ident", [P, P])
        low = sb("low", [P, 2, S])
        comb = sb("comb", [P, 2, S])
        sig = sb("sig", [P, S])
        hid = sb("hid", [P, S])
        stats = sb("stats", [P, TOK, COL_GROUPS * 6])
        small = sb("small", [P, 28])
        ln1_gb = sb("ln1_gb", [P, 2, KD])

        def at(base):
            offset = [base]

            def place(name, shape, dt=F32):
                t = nc.alloc_sbuf_tensor_at(name, shape, dt, offset=offset[0])
                offset[0] += int(np.prod(shape[1:])) * 4
                return t
            return place

        place = at(base_a)
        q_t = place("q_t", [P, 2, GH, S])
        k_t = place("k_t", [P, 2, GH, S])
        v_n = place("v_n", [P, 2, TOK, GH * HD])
        score = place("score", [P, KEYS])
        work = place("work", [P, KEYS])
        key_bias = place("key_bias", [P, KEYS])
        top8 = place("top8", [P, TOK, 8])
        place = at(base_r)
        o_t = place("o_t", [P, HEADS, 2, S], F32R)
        PROJ = Q_RANK + KV_RANK + 2 * IDX_DIM + IDX_HEADS
        proj = place("proj", [P, TOK, PROJ])
        cq_t = place("cq_t", [P, KQ, 2, S], F32R)
        ckv_t = place("ckv_t", [P, KV, 2, S], F32R)
        kidx_t = place("kidx_t", [P, S])
        qidx_t = place("qidx_t", [P, IDX_HEADS * IDX_DIM // P, S])
        relu = place("relu", [P, RELU, KEYS])
        neg_s = place("neg_s", [P, 2, KEYS])
        prob = place("prob", [P, 3, KEYS])
        prob_t = place("prob_t", [P, 2, KEYS])
        sq = place("sq", [P, Q_RANK])
        rms_g = place("rms_g", [P, KQ + KV])
        ln1_rows = at(base_r + (KF * 2 * S - 2 * D) * 4)("ln1_rows", [P, 2, D])
        ln2_rows = at(base_a)("ln2_rows", [P, 2, D])

        ssq = small[:, 0:4]
        rms_v = small[:, 4:8]
        rstd4 = small[:, 8:12]
        rms_r = small[:, 24:28]
        mean_var = small[:, 12:16]
        ln_v = small[:, 16:18]
        ln_s = small[:, 18:20]
        ln_r = small[:, 20:22]
        ln_nmr = small[:, 22:24]
        table_in = sb("table_in", [P, 2])
        row_min = sb("row_min", [P, 2, TOK])
        row_sum = sb("row_sum", [P, 2, TOK])
        row_inv = sb("row_inv", [P, 2, TOK])

        acc = ctx.enter_context(nc.psum_tensor("acc", [P, 4, 512], F32))
        tp = ctx.enter_context(nc.psum_tensor("tp", [P, 4, 512], F32))

        raw_full = [sem(f"raw_full{i}") for i in range(RING)]
        first_full = [sem(f"first_full{i}") for i in range(2)]
        const_full = sem("const_full")
        table_set = sem("table_set")
        rms_full = sem("rms_full")
        xn_full = sem("xn_full")
        ln1_rows_full = sem("ln1_rows_full")
        ln2_rows_full = sem("ln2_rows_full")
        out_done = sem("out_done")
        hi_done = sem("hi_done")
        lo_done = sem("lo_done")
        pe_used = sem("pe_used")
        ident_done = sem("ident_done")
        ssq_done = sem("ssq_done")
        rms_var = sem("rms_var")
        rms_sqrt = sem("rms_sqrt")
        rms_inv = sem("rms_inv")
        proj_done = sem("proj_done")
        proj_q_done = sem("proj_q_done")
        proj_t = sem("proj_t")
        c_hi = sem("c_hi")
        c_lo = sem("c_lo")
        in_t0_full = sem("in_t0_full")
        acc_full = sem("acc_full")
        acc_t0_full = sem("acc_t0_full")
        low_done = sem("low_done")
        comb_done = sem("comb_done")
        logits_full = sem("logits_full")
        relu_done = sem("relu_done")
        score_step = sem("score_step")
        score_masked = sem("score_masked")
        top_step = sem("top_step")
        bias_raw = sem("bias_raw")
        bias_done = sem("bias_done")
        qk_full = sem("qk_full")
        neg_done = sem("neg_done")
        min_done = sem("min_done")
        exp_done = sem("exp_done")
        inv_done = sem("inv_done")
        prob_done = sem("prob_done")
        pt_full = sem("pt_full")
        pt_done = sem("pt_done")
        pv_full = sem("pv_full")
        o_hi = sem("o_hi")
        o_lo = sem("o_lo")
        res_done = sem("res_done")
        stat_done = sem("stat_done")
        aggr_done = sem("aggr_done")
        var_done = sem("var_done")
        sqrt_done = sem("sqrt_done")
        rstd_done = sem("rstd_done")
        xhat_done = sem("xhat_done")
        xhat_act = sem("xhat_act")
        xt_full = sem("xt_full")
        xt_hi = sem("xt_hi")
        xt_val = sem("xt_val")
        xt_lo = sem("xt_lo")
        xt_lo_pool = sem("xt_lo_pool")
        ffn_full = sem("ffn_full")
        ffn_low = sem("ffn_low")
        ffn_comb = sem("ffn_comb")
        ffn_sig = sem("ffn_sig")
        ffn_hid = sem("ffn_hid")
        ffn_hi = sem("ffn_hi")
        ffn_lo = sem("ffn_lo")
        x1_step = sem("x1_step")
        nmr_done = sem("nmr_done")
        y_norm = sem("y_norm")
        y_gain = sem("y_gain")
        y_done = sem("y_done")
        y_scaled = sem("y_scaled")
        y_own_done = sem("y_own_done")

        block = ctx.enter_context(nc.Block())

        in_raw = {b: n for n, b in enumerate(IN_BLOCKS)}
        hid_flat = hid_t[:].rearrange("p k h s -> p (k h s)")

        def flat(name):
            return a[name].rearrange("n p e -> (n p) e")

        w_out_rows, w_gu_rows, w_down_rows = flat("w_out"), flat("w_gu"), flat("w_down")

        def used_out(g, h):
            n = OUT_HALVES - 1
            return (pe_used, KD + n * g + h + 1) if h < n else (acc_full, M_OUT + g + 1)

        def used_ffn(tile, j):
            return (pe_used, USED_FFN + 3 * tile + j + 1) if j < 3 else (ffn_full, tile + 1)

        def used_down(g, h):
            n = len(DOWN_K) - 1
            return (pe_used, USED_DOWN + n * g + h + 1) if h < n else (acc_full, M_DOWN + g + 1)

        def used_static(v):
            if v < 2 * R_QIDX:
                return pe_used, sum(1 for b in IN_BLOCKS for h in (0, 1) if 2 * b + h <= v)
            if v < 2 * R_GROUP:
                return acc_full, 2 * (v - 2 * R_QIDX) + 2
            if v < 2 * R_OUT:
                g, j = divmod(v - 2 * R_GROUP, 4)
                return acc_full, M_GROUP + g * M_PER_GROUP + (2, 4, 8, 10)[j]
            return used_out(*divmod(v - 2 * R_OUT, OUT_HALVES))

        @block.sync
        def _(sp):
            def load(r, slot, dst_elems, src, first=False, late=0):
                if not first:
                    sp.wait_ge(lo_done, len(SPLIT_ORDER) if isinstance(r, int) and r == 4 else 2 * r - 6 + late)
                sp.dma_start(raw[:, slot, 0:dst_elems], src).then_inc(raw_full[slot], 16)

            for v in SPLIT_ORDER:
                r, half = divmod(v, 2)
                src = a["x_t"][0] if r in X_BLOCKS else a["w_in"][0]
                n = HALF if r in X_BLOCKS else W_IN
                full = raw_full[r] if half == 1 else first_full[r]
                sp.dma_start(raw[:, r, half * n:(half + 1) * n], src[:, half * n:(half + 1) * n])\
                    .then_inc(full, 16)

            def rows(dst, first, full):
                for n in range(2):
                    row = a["ln_rows"][first + n:first + n + 1, :].broadcast_to([P, D])
                    sp.dma_start(dst[:, n, :], row).then_inc(full, 16)

            for r in range(len(SPLIT_ORDER) // 2, R_QIDX):
                if r in X_BLOCKS:
                    load(r, r % RING, RAW_ELEMS, a["x_t"][X_BLOCKS.index(r)], first=r < RING)
                else:
                    load(r, r % RING, 2 * W_IN, a["w_in"][in_raw[r]], first=r < RING)
            for n in range(2):
                load(R_QIDX + n, (R_QIDX + n) % RING, RAW_ELEMS, a["w_qidx"][n])
            for g in range(GROUPS):
                r = R_GROUP + 2 * g
                load(r, r % RING, RAW_ELEMS, a["w_uq"][g])
                load(r + 1, (r + 1) % RING, RAW_ELEMS, a["w_ukv"][g])
                if g == 0:
                    sp.dma_start(xn[:], a["x"].rearrange("(t p) d -> p t d", p=P)).then_inc(xn_full, 16)
            with sp.Fori(0, COL_GROUPS) as g:
                for j in range(RING):
                    load(R_OUT + RING * g + j, j, RAW_ELEMS,
                         w_out_rows[bass.ds(g * P, P), j * RAW_ELEMS:(j + 1) * RAW_ELEMS])
            sp.wait_ge(pv_full, HEADS)
            rows(ln1_rows, 0, ln1_rows_full)
            with sp.Fori(0, KF // 2) as i:
                for j in range(RING):
                    load(R_FFN + i * RING + j, j, RAW_ELEMS, w_gu_rows[bass.ds((i * RING + j) * P, P), :],
                         late=1)

            def load_down(g, b):
                k0, k1 = DOWN_K0[2 * b], DOWN_K0[2 * b] + DOWN_K[2 * b] + DOWN_K[2 * b + 1]
                load(R_DOWN + DOWN_BLOCKS * g + b, b % RING, (k1 - k0) * GC,
                     w_down_rows[bass.ds(g * P, P), k0 * GC:k1 * GC])

            for b in range(RING):
                load_down(0, b)
            sp.wait_ge(ffn_full, KF)
            rows(ln2_rows, 2, ln2_rows_full)
            for b in range(RING, DOWN_BLOCKS):
                load_down(0, b)
            with sp.Fori(1, COL_GROUPS) as g:
                for b in range(DOWN_BLOCKS):
                    load_down(g, b)
            for own, n in Y_ORDER:
                if own:
                    sp.wait_ge(y_own_done, n + 1)
                else:
                    sp.wait_ge(y_done, n + 1)
                c, t = (Y_OWN if own else Y_SHARED)[n]
                sp.dma_start(a["out"][t * P:(t + 1) * P, c * 512:(c + 1) * 512],
                             xn[:, t, c * 512:(c + 1) * 512]).then_inc(out_done, 16)
            sp.wait_ge(out_done, 16 * 8)

        @block.scalar
        def _(act):
            act.wait_ge(table_set, 1)
            act.dma_start(ln1_gb[:], a["ln1_gb_t"]).then_inc(const_full, 16)

            def hi_static(v):
                r, half = divmod(v, 2)
                if v in SPLIT_ORDER:
                    act.wait_ge(raw_full[r] if half == 1 else first_full[r], 16)
                elif half == 0:
                    act.wait_ge(raw_full[r % RING], 16 * (r // RING + 1))
                if r in X_BLOCKS:
                    k0 = 8 * X_BLOCKS.index(r) + 4 * half
                    src = raw[:, r % RING, half * HALF:(half + 1) * HALF].rearrange("p (k s) -> p k s", s=S)
                    act.activation(act_t[:, k0:k0 + 4, 0, :], src, ACT.Copy).then_inc(hi_done, 1)
                    return
                w = ring_index(v)
                if w >= RING:
                    prev = next(u for u in range(v) if ring_index(u) == w - RING and u // 2 not in X_BLOCKS)
                    act.wait_ge(*used_static(prev))
                n = W_IN if r < R_QIDX else HALF
                act.activation(w_hi[:, w % RING, 0:n], raw[:, r % RING, half * n:(half + 1) * n],
                               ACT.Copy).then_inc(hi_done, 1)

            def take_low(m):
                act.wait_ge(acc_full, m + 1)
                if m >= 2:
                    act.wait_ge(comb_done, m - 1)
                act.activation(low[:, m % 2, :], acc[:, m % 4, S:2 * S], ACT.Copy).then_inc(low_done, 1)

            def load_table(func):
                act.activation(table_in[:, 1:2], table_in[:, 0:1], func)

            for v in SPLIT_ORDER + tuple(range(len(SPLIT_ORDER), 2 * R_QIDX)):
                hi_static(v)
            hi_static(2 * R_QIDX)
            hi_static(2 * R_QIDX + 1)

            load_table(ACT.Sqrt)
            for t in range(TOK):
                if t == 0:
                    act.wait_ge(in_t0_full, 1)
                else:
                    act.wait_ge(pe_used, KD)
                act.activation(sq[:, 0:Q_RANK], acc[:, 2 * t, :], ACT.Square,
                               accum_out=ssq[:, 2 * t:2 * t + 1]).then_inc(ssq_done, 1)
                act.wait_ge(ssq_done, 2 * t + 1)
                act.activation(sq[:, 0:KV_RANK], acc[:, 2 * t + 1, 0:KV_RANK], ACT.Square,
                               accum_out=ssq[:, 2 * t + 1:2 * t + 2]).then_inc(ssq_done, 1)
                act.wait_ge(ssq_done, 2 * t + 2)
            act.wait_ge(rms_var, 2)
            act.activation(rms_v, rstd4, ACT.Sqrt).then_inc(rms_sqrt, 1)
            for t in range(TOK):
                c = Q_RANK + KV_RANK
                act.activation(proj[:, t, c:c + IDX_DIM], acc[:, 2 * t + 1, KV_RANK:KV_RANK + IDX_DIM],
                               ACT.Copy).then_inc(proj_done, 1)
                act.activation(proj[:, t, c + IDX_DIM:c + 2 * IDX_DIM + IDX_HEADS],
                               acc[:, 2 * t + 1, KV_RANK:KV_RANK + IDX_DIM + IDX_HEADS],
                               ACT.Copy).then_inc(proj_done, 1)
            act.wait_ge(rms_inv, 4)
            for t in range(TOK):
                act.activation(proj[:, t, Q_RANK:Q_RANK + KV_RANK], acc[:, 2 * t + 1, 0:KV_RANK], ACT.Copy,
                               scale=rstd4[:, 2 * t + 1:2 * t + 2]).then_inc(proj_done, 1)
            act.wait_ge(rms_full, 16)
            act.wait_ge(const_full, 16)
            for n in range(KQ + KV):
                act.wait_ge(proj_t, (n | 1) + 1)
                dst = cq_t[:, n, 0, :] if n < KQ else ckv_t[:, n - KQ, 0, :]
                act.activation(dst, tp[:, n // 2, (n % 2) * S:(n % 2 + 1) * S], ACT.Copy,
                               scale=rms_g[:, n:n + 1]).then_inc(c_hi, 1)
            act.wait_ge(proj_t, KQ + KV + 1)
            act.activation(kidx_t[:], tp[:, 3, 0:S], ACT.Copy).then_inc(c_hi, 1)
            hi_static(2 * R_QIDX + 2)
            hi_static(2 * R_QIDX + 3)
            for m in range(M_GROUP):
                take_low(m)
                if m % 2 == 1:
                    hi_static(2 * R_GROUP + m // 2)
            for h in range(IDX_HEADS):
                act.wait_ge(logits_full, h + 1)
                if h >= RELU:
                    act.wait_ge(score_step, 2 * (h - RELU + 1))
                act.activation(relu[:, h % RELU, :], tp[:, h % 4, 0:KEYS], ACT.Relu,
                               scale=IDX_SCALE).then_inc(relu_done, 1)

            def piece(s):
                g, j = divmod(s, 4)
                m0 = M_GROUP + g * M_PER_GROUP
                if j < 3:
                    for m in {0: (0, 1), 1: (2, 3), 2: (4, 5, 6, 7)}[j]:
                        take_low(m0 + m)
                else:
                    for t in range(TOK):
                        m = m0 + 8 + t
                        act.wait_ge(acc_full, m + 1)
                        act.activation(v_n[:, g % 2, t, 0:S], acc[:, m % 4, 0:S], ACT.Copy)\
                           .then_inc(low_done, 1)

            for s in range(4):
                piece(s)
                hi_static(2 * R_GROUP + 4 + s)
            for s in range(HEADS + 4):
                if s >= 4:
                    act.wait_ge(pv_full, s - 3)
                    act.activation(o_t[:, s - 4, 0, :], tp[:, 3, 0:S], ACT.Copy).then_inc(o_hi, 1)
                if 3 <= s < HEADS + 3:
                    act.wait_ge(pt_full, s - 2)
                    act.activation(prob_t[:, (s - 3) % 2, :], tp[:, 2, 0:KEYS], ACT.Copy).then_inc(pt_done, 1)
                if s < HEADS:
                    for t in range(TOK):
                        act.wait_ge(min_done, 2 * s + t + 1)
                        cols = slice(0, P) if t == 0 else slice(P, KEYS)
                        act.activation(prob[:, s % 3, cols], neg_s[:, s % 2, cols], ACT.Exp, scale=-1.0,
                                       bias=row_min[:, s % 2, t:t + 1],
                                       accum_out=row_sum[:, s % 2, t:t + 1]).then_inc(exp_done, 1)
                if s + 4 < HEADS:
                    piece(s + 4)
                    hi_static(2 * R_GROUP + 8 + s)
                if s in (HEADS, HEADS + 1):
                    hi_static(2 * R_OUT + 4 + s - HEADS)

            def hi_loop(used, raw_count, half, slot, n=HALF, first=None):
                first = half * n if first is None else first
                if half == 0:
                    act.wait_ge(raw_full[slot], 16 * raw_count)
                act.wait_ge(*used)
                act.activation(w_hi[:, (2 * slot + half) % RING, 0:n], raw[:, slot, first:first + n],
                               ACT.Copy).then_inc(hi_done, 1)

            def out_half(h, g):
                hi_loop(used_out(g, h - 4) if h >= 4 else used_out(g - 1, h + 4), R_OUT // RING + 1 + g,
                        h % 2, h // 2)

            out_half(6, 0)
            out_half(7, 0)
            with act.Fori(1, COL_GROUPS) as g:
                for h in range(OUT_HALVES):
                    out_half(h, g)
            def hi_first(j):
                if j < 2:
                    act.wait_ge(raw_full[j], 16 * (R_FFN // RING + 1))
                act.wait_ge(*used_out(COL_GROUPS - 1, j + 4))
                act.activation(w_hi[:, j, :], raw[:, j % 2, (j // 2) * HALF:(j // 2 + 1) * HALF],
                               ACT.Copy).then_inc(hi_done, 1)

            hi_first(0)
            hi_first(1)
            hi_first(2)
            load_table(ACT.Sqrt)

            act.wait_ge(var_done, 1)
            act.activation(ln_s, ln_v, ACT.Sqrt).then_inc(sqrt_done, 1)
            act.wait_ge(nmr_done, 1)
            for c in range(ACT_XHAT):
                part = xn[:, 1, c * 512:(c + 1) * 512]
                act.activation(part, part, ACT.Identity, scale=ln_r[:, 1:2], bias=ln_nmr[:, 1:2])\
                   .then_inc(xhat_act, 1)
            for k in range(KD):
                if k == 2:
                    hi_first(3)
                act.wait_ge(xt_full, (k | 1) + 1)
                act.activation(act_t[:, k, 0, :], tp[:, (k // 2) % 4, (k % 2) * S:(k % 2 + 1) * S],
                               ACT.Identity, scale=ln1_gb[:, 0, k:k + 1],
                               bias=ln1_gb[:, 1, k:k + 1]).then_inc(xt_hi, 1)

            def ffn_low_step(tile, c):
                act.wait_ge(ffn_full, tile + 1)
                act.activation(low[:], acc[:, 2 * c:2 * c + 2, S:2 * S], ACT.Copy).then_inc(ffn_low, 1)

            def ffn_silu_step(tile):
                act.wait_ge(ffn_comb, tile + 1)
                act.activation(sig[:], comb[:, 0, :], ACT.Silu).then_inc(ffn_sig, 1)

            def ffn_hi_step(tile):
                act.wait_ge(ffn_hid, tile + 1)
                act.activation(hid_flat[:, bass.ds(tile * 2 * S, S)], hid[:], ACT.Copy).then_inc(ffn_hi, 1)

            def ffn_tile(c, i, older=True):
                tile = 2 * i + c
                for j in range(4):
                    hi_loop(used_ffn(tile - 1, j), R_FFN // RING + 1 + i, j % 2, 2 * c + j // 2)
                    if j == 0 and older:
                        ffn_silu_step(tile - 2)
                    if j == 1 and older:
                        ffn_hi_step(tile - 2)
                ffn_low_step(tile - 1, 1 - c)

            ffn_tile(1, 0, older=False)
            with act.Fori(1, KF // 4) as i:
                ffn_tile(0, i)
                ffn_tile(1, i)
            act.wait_ge(x1_step, 16)
            with act.Fori(KF // 4, KF // 2) as i:
                ffn_tile(0, i)
                ffn_tile(1, i)

            def down_half(h, g):
                n = len(DOWN_K)
                used = used_down(g, h - 4) if h >= 4 else \
                    used_ffn(KF - 1, h) if isinstance(g, int) and g == 0 else used_down(g - 1, h + n - 4)
                hi_loop(used, R_DOWN // RING + 1 + DOWN_BLOCKS // RING * g + h // 8, h % 2, h // 2 % RING,
                        n=DOWN_K[h] * GC, first=h % 2 * HALF)

            for h in range(len(DOWN_K)):
                down_half(h, 0)
                if h == 0:
                    ffn_silu_step(KF - 2)
                if h == 1:
                    ffn_hi_step(KF - 2)
                if h == 3:
                    ffn_low_step(KF - 1, 1)
                    ffn_silu_step(KF - 1)
                    ffn_hi_step(KF - 1)
            with act.Fori(1, COL_GROUPS) as g:
                for h in range(len(DOWN_K)):
                    down_half(h, g)

            load_table(ACT.Sqrt)
            act.wait_ge(var_done, 2)
            act.activation(ln_s, ln_v, ACT.Sqrt).then_inc(sqrt_done, 1)
            act.wait_ge(nmr_done, 2)
            for c, t in Y_SHARED:
                part = xn[:, t, c * 512:(c + 1) * 512]
                act.activation(part, part, ACT.Identity, scale=ln_r[:, t:t + 1],
                               bias=ln_nmr[:, t:t + 1]).then_inc(y_norm, 1)

        @block.vector
        def _(dve):
            def lo_static(v):
                r, half = divmod(v, 2)
                dve.wait_ge(hi_done, SPLIT_PLACE.get(v, v) + 1)
                if r in X_BLOCKS:
                    k0 = 8 * X_BLOCKS.index(r) + 4 * half
                    src = raw[:, r % RING, half * HALF:(half + 1) * HALF].rearrange("p (k s) -> p k s", s=S)
                    dve.tensor_tensor(act_t[:, k0:k0 + 4, 1, :], src, act_t[:, k0:k0 + 4, 0, :],
                                      ALU.subtract).then_inc(lo_done, 1)
                    return
                w = ring_index(v)
                n = W_IN if r < R_QIDX else HALF
                dve.tensor_tensor(w_lo[:, w % RING, 0:n], raw[:, r % RING, half * n:(half + 1) * n],
                                  w_hi[:, w % RING, 0:n], ALU.subtract).then_inc(lo_done, 1)

            def combine(m, dst):
                dve.wait_ge(low_done, m + 1)
                dve.tensor_tensor(dst, acc[:, m % 4, 0:S], low[:, m % 2, :], ALU.add).then_inc(comb_done, 1)

            for v in SPLIT_ORDER + tuple(range(len(SPLIT_ORDER), 2 * R_QIDX + 2)):
                lo_static(v)

            dve.wait_ge(ssq_done, 4)
            for n, width in enumerate((Q_RANK, KV_RANK)):
                dve.tensor_scalar(rstd4[:, n:4:2], ssq[:, n:4:2], 1.0 / width, EPS, ALU.mult, ALU.add)\
                   .then_inc(rms_var, 1)
            dve.wait_ge(rms_sqrt, 1)
            dve.reciprocal(rms_r, rms_v).then_inc(rms_inv, 1)
            dve.wait_ge(rms_inv, 1)
            dve.tensor_tensor(rms_v, rms_r, rms_r, ALU.mult).then_inc(rms_inv, 1)
            dve.wait_ge(rms_inv, 2)
            dve.scalar_tensor_tensor(out=rms_v, in0=rms_v, scalar=-0.5, in1=rstd4, op0=ALU.mult,
                                     op1=ALU.mult).then_inc(rms_inv, 1)
            dve.wait_ge(rms_inv, 3)
            dve.scalar_tensor_tensor(out=rstd4, in0=rms_v, scalar=1.5, in1=rms_r, op0=ALU.add,
                                     op1=ALU.mult).then_inc(rms_inv, 1)
            dve.wait_ge(rms_inv, 4)
            for t in range(TOK):
                dve.tensor_scalar(proj[:, t, 0:Q_RANK], acc[:, 2 * t, :], rstd4[:, 2 * t:2 * t + 1], None,
                                  ALU.mult).then_inc(proj_q_done, 1)
            for n in range(KQ + KV):
                dve.wait_ge(c_hi, (n | 1) + 1)
                hi_, lo_ = (cq_t[:, n, 0, :], cq_t[:, n, 1, :]) if n < KQ else \
                    (ckv_t[:, n - KQ, 0, :], ckv_t[:, n - KQ, 1, :])
                dve.scalar_tensor_tensor(out=lo_, in0=tp[:, n // 2, (n % 2) * S:(n % 2 + 1) * S],
                                         scalar=rms_g[:, n:n + 1], in1=hi_, op0=ALU.mult,
                                         op1=ALU.subtract).then_inc(c_lo, 1)
            lo_static(2 * R_QIDX + 2)
            lo_static(2 * R_QIDX + 3)
            for m in range(M_GROUP):
                combine(m, qidx_t[:, m, :])
                if m % 2 == 1:
                    lo_static(2 * R_GROUP + m // 2)

            w0 = Q_RANK + KV_RANK + 2 * IDX_DIM
            blocks = ((0, slice(0, P)), (1, slice(P, KEYS)))
            for h in range(IDX_HEADS):
                dve.wait_ge(relu_done, h + 1)
                for t, cols in blocks:
                    w_idx = proj[:, t, w0 + h:w0 + h + 1]
                    if h == 0:
                        dve.tensor_scalar(score[:, cols], relu[:, 0, cols], w_idx, None, ALU.mult)\
                           .then_inc(score_step, 1)
                    else:
                        dve.wait_ge(score_step, 2 * (h - 1) + t + 1)
                        dve.scalar_tensor_tensor(out=score[:, cols], in0=relu[:, h % RELU, cols], scalar=w_idx,
                                                 in1=score[:, cols], op0=ALU.mult, op1=ALU.add)\
                           .then_inc(score_step, 1)

            def piece(s):
                g, j = divmod(s, 4)
                m0 = M_GROUP + g * M_PER_GROUP
                if j < 2:
                    for n in range(2):
                        combine(m0 + 2 * j + n, q_t[:, g % 2, 2 * j + n, :])
                elif j == 2:
                    for n in range(GH):
                        combine(m0 + GH + n, k_t[:, g % 2, n, :])
                else:
                    for t in range(TOK):
                        m = m0 + 2 * GH + t
                        dve.wait_ge(low_done, m + 1)
                        dve.tensor_copy(v_n[:, g % 2, t, S:2 * S], acc[:, m % 4, S:2 * S]).then_inc(comb_done, 1)

            dve.wait_ge(score_masked, 2)
            for n in range(TOPK // 8):
                src = score if n == 0 else work
                if n > 0:
                    dve.wait_ge(top_step, 4 * n)
                for t, cols in blocks:
                    dve.max(top8[:, t, :], src[:, cols]).then_inc(top_step, 1)
                for t, cols in blocks:
                    dve.wait_ge(top_step, 4 * n + t + 1)
                    dve.match_replace(work[:, cols], top8[:, t, :], src[:, cols], TAKEN).then_inc(top_step, 1)
                if n in PIECE_AT:
                    piece(PIECE_AT.index(n))
            dve.wait_ge(top_step, 4 * (TOPK // 8))
            dve.tensor_scalar(key_bias[:], work[:], NOT_TAKEN, MASKED, ALU.is_gt, ALU.mult).then_inc(bias_raw, 1)
            dve.wait_ge(bias_done, 2)

            for s in range(HEADS + 4):
                if s >= 4:
                    dve.wait_ge(o_hi, s - 3)
                    dve.tensor_tensor(o_t[:, s - 4, 1, :], tp[:, 3, 0:S], o_t[:, s - 4, 0, :],
                                      ALU.subtract).then_inc(o_lo, 1)
                if s < HEADS:
                    dve.wait_ge(qk_full, s + 1)
                    dve.scalar_tensor_tensor(out=neg_s[:, s % 2, :], in0=tp[:, s % 2, 0:KEYS],
                                             scalar=-ATTN_SCALE, in1=key_bias[:], op0=ALU.mult,
                                             op1=ALU.add).then_inc(neg_done, 1)
                    if s >= 1:
                        dve.wait_ge(exp_done, 2 * s)
                        if s >= 3:
                            dve.wait_ge(prob_done, 2 * (s - 2))
                        dve.reciprocal(row_inv[:, s % 2, :], row_sum[:, (s - 1) % 2, :]).then_inc(inv_done, 1)
                    dve.wait_ge(neg_done, s + 1)
                    for t, cols in blocks:
                        dve.tensor_reduce(row_min[:, s % 2, t:t + 1], neg_s[:, s % 2, cols], AX.X, ALU.min)\
                           .then_inc(min_done, 1)
                if s == HEADS:
                    dve.wait_ge(exp_done, 2 * s)
                    dve.wait_ge(prob_done, 2 * (s - 2))
                    dve.reciprocal(row_inv[:, s % 2, :], row_sum[:, (s - 1) % 2, :]).then_inc(inv_done, 1)
                if 1 <= s <= HEADS - 4:
                    if s == 1:
                        dve.wait_ge(lo_done, 2 * R_GROUP + 8)
                    lo_static(2 * R_GROUP + 7 + s)
                if POOL_NORM < s <= HEADS:
                    dve.wait_ge(inv_done, s)
                    dve.wait_ge(prob_done, 2 * (s - 1))
                    for t, cols in blocks:
                        dve.tensor_scalar(prob[:, (s - 1) % 3, cols], prob[:, (s - 1) % 3, cols],
                                          row_inv[:, s % 2, t:t + 1], None, ALU.mult).then_inc(prob_done, 1)
                if s + 4 < HEADS:
                    piece(s + 4)
                if s in (HEADS, HEADS + 1):
                    lo_static(2 * R_OUT + 4 + s - HEADS)

            def lo_loop(v, half, slot, n=HALF, first=None):
                first = half * n if first is None else first
                dve.wait_ge(hi_done, v + 1)
                h = (2 * slot + half) % RING
                dve.tensor_tensor(w_lo[:, h, 0:n], raw[:, slot, first:first + n], w_hi[:, h, 0:n],
                                  ALU.subtract).then_inc(lo_done, 1)

            def residual(g, t, m0, n0):
                part = xn[:, t, g * GC:(g + 1) * GC]
                if t == 0:
                    dve.wait_ge(acc_t0_full, m0 - M_OUT + g + 1)
                else:
                    dve.wait_ge(acc_full, m0 + g + 1)
                dve.scalar_tensor_tensor(out=part, in0=part, scalar=ALPHA, in1=acc[:, 2 * (g % 2) + t, :],
                                         op0=ALU.mult, op1=ALU.add).then_inc(res_done, 1)
                dve.wait_ge(res_done, n0 + TOK * g + t + 1)
                dve.bn_stats(stats[:, t, 6 * g:6 * g + 6], part).then_inc(stat_done, 1)

            dve.wait_ge(xn_full, 16)
            for g in range(COL_GROUPS):
                for h in range(6 if g == 0 else 0, OUT_HALVES):
                    lo_loop(2 * R_OUT + OUT_HALVES * g + h, h % 2, h // 2)
                    if g > 0 and h in (2, 4):
                        residual(g - 1, h // 2 - 1, M_OUT, 0)

            def lo_first(j):
                dve.wait_ge(hi_done, 2 * R_FFN + j + 1)
                dve.tensor_tensor(w_lo[:, j, :], raw[:, j % 2, (j // 2) * HALF:(j // 2 + 1) * HALF],
                                  w_hi[:, j, :], ALU.subtract).then_inc(lo_done, 1)

            for j in range(3):
                lo_first(j)
            for t in range(TOK):
                residual(COL_GROUPS - 1, t, M_OUT, 0)

            def row_stats(which):
                dve.wait_ge(stat_done, TOK * COL_GROUPS * which)
                for t in range(TOK):
                    dve.bn_aggr(mean_var[:, 2 * t:2 * t + 2], stats[:, t, :])\
                   .then_inc(aggr_done, 1)
                dve.wait_ge(aggr_done, TOK * which)
                dve.tensor_scalar(ln_v, mean_var[:, 1:4:2], EPS, None, ALU.add).then_inc(var_done, 1)
                dve.wait_ge(sqrt_done, which)
                dve.reciprocal(ln_r, ln_s).then_inc(rstd_done, 1)
                dve.wait_ge(rstd_done, which)

            def shift():
                dve.scalar_tensor_tensor(out=ln_nmr, in0=mean_var[:, 0:4:2], scalar=-1.0, in1=ln_r,
                                         op0=ALU.mult, op1=ALU.mult).then_inc(nmr_done, 1)

            row_stats(1)
            shift()
            for c in range(4):
                for t in range(1 if c < ACT_XHAT else TOK):
                    part = xn[:, t, c * 512:(c + 1) * 512]
                    dve.tensor_scalar(part, part, mean_var[:, 2 * t:2 * t + 1], ln_r[:, t:t + 1],
                                      ALU.subtract, ALU.mult).then_inc(xhat_done, 1)
            vals = (low, comb)

            def value(k):
                dve.wait_ge(xt_hi, (k | 1) + 1)
                if k - 4 in POOL_LO:
                    dve.wait_ge(xt_lo_pool, len([u for u in POOL_LO if u <= k - 4]))
                dve.tensor_scalar(vals[(k // 2) % 2][:, k % 2, :],
                                  tp[:, (k // 2) % 4, (k % 2) * S:(k % 2 + 1) * S],
                                  ln1_gb[:, 0, k:k + 1], ln1_gb[:, 1, k:k + 1], ALU.mult, ALU.add)\
                    .then_inc(xt_val, 1)

            def value_lo(k):
                if k not in POOL_LO:
                    dve.wait_ge(xt_val, k + 1)
                    dve.tensor_tensor(act_t[:, k, 1, :], vals[(k // 2) % 2][:, k % 2, :], act_t[:, k, 0, :],
                                      ALU.subtract).then_inc(xt_lo, 1)

            for k in range(0, KD, 2):
                value(k)
                value(k + 1)
                value_lo(k)
                value_lo(k + 1)
            dve.wait_ge(lo_done, 2 * R_FFN + 4)

            def ffn_combine(tile, c):
                dve.wait_ge(ffn_low, tile + 1)
                dve.tensor_tensor(comb[:], acc[:, 2 * c:2 * c + 2, 0:S], low[:], ALU.add).then_inc(ffn_comb, 1)

            def ffn_mul(tile):
                dve.wait_ge(ffn_sig, tile + 1)
                dve.tensor_tensor(hid[:], sig[:], comb[:, 1, :], ALU.mult).then_inc(ffn_hid, 1)

            def ffn_lo_step(tile):
                dve.wait_ge(ffn_hi, tile + 1)
                dve.tensor_tensor(hid_flat[:, bass.ds(tile * 2 * S + S, S)], hid[:],
                                  hid_flat[:, bass.ds(tile * 2 * S, S)], ALU.subtract).then_inc(ffn_lo, 1)

            def ffn_tile(c, i, older=True):
                tile = 2 * i + c
                for j in range(4):
                    lo_loop(2 * R_FFN + 4 * tile + j, j % 2, 2 * c + j // 2)
                    if j == 0 and older:
                        ffn_mul(tile - 2)
                    if j == 1 and older:
                        ffn_lo_step(tile - 2)
                ffn_combine(tile - 1, 1 - c)

            ffn_tile(1, 0, older=False)
            with dve.Fori(1, KF // 4) as i:
                ffn_tile(0, i)
                ffn_tile(1, i)
            dve.wait_ge(x1_step, 16)
            with dve.Fori(KF // 4, KF // 2) as i:
                ffn_tile(0, i)
                ffn_tile(1, i)

            for g in range(COL_GROUPS):
                for h in range(len(DOWN_K)):
                    lo_loop(2 * R_DOWN + len(DOWN_K) * g + h, h % 2, h // 2 % RING,
                            n=DOWN_K[h] * GC, first=h % 2 * HALF)
                    if g == 0 and h == 0:
                        ffn_mul(KF - 2)
                    if g == 0 and h == 1:
                        ffn_lo_step(KF - 2)
                    if g == 0 and h == 3:
                        ffn_combine(KF - 1, 1)
                        ffn_mul(KF - 1)
                        ffn_lo_step(KF - 1)
                    if g > 0 and h in (2, 4):
                        residual(g - 1, h // 2 - 1, M_DOWN, TOK * COL_GROUPS)
            for t in range(TOK):
                residual(COL_GROUPS - 1, t, M_DOWN, TOK * COL_GROUPS)

            row_stats(2)
            shift()
            dve.wait_ge(ln2_rows_full, 32)
            def y_own(n):
                c, t = Y_OWN[n]
                part = xn[:, t, c * 512:(c + 1) * 512]
                dve.scalar_tensor_tensor(out=part, in0=part, scalar=mean_var[:, 2 * t:2 * t + 1],
                                         in1=ln2_rows[:, 0, c * 512:(c + 1) * 512], op0=ALU.subtract,
                                         op1=ALU.mult).then_inc(y_scaled, 1)
                dve.wait_ge(y_scaled, n + 1)
                dve.scalar_tensor_tensor(out=part, in0=part, scalar=ln_r[:, t:t + 1],
                                         in1=ln2_rows[:, 1, c * 512:(c + 1) * 512], op0=ALU.mult,
                                         op1=ALU.add).then_inc(y_own_done, 1)

            def y_shared(n):
                c, t = Y_SHARED[n]
                part = xn[:, t, c * 512:(c + 1) * 512]
                dve.wait_ge(y_norm, n + 1)
                dve.tensor_tensor(part, part, ln2_rows[:, 0, c * 512:(c + 1) * 512], ALU.mult)\
                   .then_inc(y_gain, 1)

            for own, n in Y_ORDER:
                (y_own if own else y_shared)(n)

        @block.gpsimd
        def _(pool):
            pool.dma_start(rms_g[:], a["rms_g_t"]).then_inc(rms_full, 16)
            pool.memset(table_in[:], 1.0).then_inc(table_set, 1)
            pool.memset(ident[:], 0.0).then_inc(ident_done, 1)
            pool.wait_ge(ident_done, 1)
            pool.affine_select(out=ident[:], in_=ident[:], compare_op=ALU.not_equal, fill=1.0, base=0,
                               pattern=[[-1, P]], channel_multiplier=1).then_inc(ident_done, 1)
            blocks = ((0, slice(0, P), P), (1, slice(P, KEYS), S))
            pool.wait_ge(score_step, 2 * IDX_HEADS)
            for t, cols, n in blocks:
                pool.affine_select(out=score[:, cols], in_=score[:, cols], compare_op=ALU.is_ge,
                                   fill=NOT_CAUSAL, base=t * P, pattern=[[-1, n]], channel_multiplier=1)\
                    .then_inc(score_masked, 1)
            def lo_pool(v):
                pool.wait_ge(hi_done, v + 1)
                pool.wait_ge(lo_done, v)
                w = ring_index(v) % RING
                pool.tensor_tensor(w_lo[:, w, :], raw[:, v // 2 % RING, v % 2 * HALF:(v % 2 + 1) * HALF],
                                   w_hi[:, w, :], ALU.subtract).then_inc(lo_done, 1)

            for v in range(2 * R_GROUP + 4, 2 * R_GROUP + 7):
                lo_pool(v)
            pool.wait_ge(bias_raw, 1)
            for t, cols, n in blocks:
                pool.affine_select(out=key_bias[:, cols], in_=key_bias[:, cols], compare_op=ALU.is_ge,
                                   fill=MASKED, base=t * P, pattern=[[-1, n]], channel_multiplier=1)\
                    .then_inc(bias_done, 1)
            lo_pool(2 * R_GROUP + 7)
            for s in range(POOL_NORM):
                pool.wait_ge(inv_done, s + 1)
                for t, cols, n in blocks:
                    pool.tensor_scalar(prob[:, s % 3, cols], prob[:, s % 3, cols],
                                       row_inv[:, (s + 1) % 2, t:t + 1], None, ALU.mult).then_inc(prob_done, 1)
            vals = (low, comb)
            for k in POOL_LO:
                if k == POOL_LO[1]:
                    pool.wait_ge(hi_done, 2 * R_FFN + 4)
                    pool.wait_ge(lo_done, 2 * R_FFN + 3)
                    pool.tensor_tensor(w_lo[:, 3, :], raw[:, 1, HALF:RAW_ELEMS], w_hi[:, 3, :],
                                       ALU.subtract).then_inc(lo_done, 1)
                pool.wait_ge(xt_hi, k + 1)
                pool.wait_ge(xt_val, k + 1)
                pool.tensor_tensor(act_t[:, k, 1, :], vals[(k // 2) % 2][:, k % 2, :], act_t[:, k, 0, :],
                                   ALU.subtract).then_inc(xt_lo_pool, 1)
            pool.wait_ge(ln1_rows_full, 32)
            pool.wait_ge(xt_full, KD)
            n = 0
            for c in range(4):
                for t in range(TOK):
                    part = xn[:, t, c * 512:(c + 1) * 512]
                    pool.tensor_tensor(part, part, ln1_rows[:, 0, c * 512:(c + 1) * 512], ALU.mult)\
                        .then_inc(x1_step, 1)
                    n += 1
                    pool.wait_ge(x1_step, n)
                    pool.tensor_tensor(part, part, ln1_rows[:, 1, c * 512:(c + 1) * 512], ALU.add)\
                        .then_inc(x1_step, 1)
                    n += 1
            pool.wait_ge(ln2_rows_full, 32)
            for n, (c, t) in enumerate(Y_SHARED):
                part = xn[:, t, c * 512:(c + 1) * 512]
                pool.wait_ge(y_gain, n + 1)
                pool.tensor_tensor(part, part, ln2_rows[:, 1, c * 512:(c + 1) * 512], ALU.add)\
                    .then_inc(y_done, 1)

        @block.tensor
        def _(pe):
            def pair(bank, w, e0, rhs, start, stop):
                wh = w_hi[:, w, e0:e0 + P]
                wl = w_lo[:, w, e0:e0 + P]
                if start:
                    pe.matmul(acc[:, bank, :], wh, rhs, start=True, stop=False)
                    return pe.matmul(acc[:, bank, 0:S], wl, rhs[:, 0, :], start=False, stop=False,
                                     skip_group_check=True)
                pe.matmul(acc[:, bank, 0:S], wl, rhs[:, 0, :], start=False, stop=False, skip_group_check=True)
                return pe.matmul(acc[:, bank, :], wh, rhs, start=False, stop=stop)

            spans = ((0, 0, Q_RANK), (1, Q_RANK, W_IN))
            steps = [(k, t) for k in range(KD - 2) for t in range(TOK)]
            steps += [(k, t) for t in range(TOK) for k in (KD - 2, KD - 1)]
            for k, t in steps:
                v = 2 * IN_BLOCKS[k // 2] + k % 2
                w = ring_index(v) % RING
                pe.wait_ge(lo_done, SPLIT_PLACE.get(v, v) + 1)
                if k == 4 and t == 0:
                    pe.wait_ge(lo_done, len(SPLIT_ORDER))
                for x_part, w_part in ((0, w_hi), (0, w_lo), (1, w_hi)):
                    for b, c0, c1 in spans:
                        last = pe.matmul(acc[:, 2 * t + b, 0:c1 - c0],
                                         act_t[:, k, x_part, t * P:(t + 1) * P], w_part[:, w, c0:c1],
                                         start=(k == 0 and x_part == 0 and w_part is w_hi),
                                         stop=(k == KD - 1 and x_part == 1))
                if t == TOK - 1:
                    last.then_inc(pe_used, 1)
                elif k == KD - 1:
                    last.then_inc(in_t0_full, 1)
            pe.wait_ge(ident_done, 2)
            for t in range(TOK):
                for n in range(KQ + KV + 1):
                    if n == 0:
                        pe.wait_ge(proj_q_done, t + 1)
                    if n == KQ:
                        pe.wait_ge(proj_done, 2 * TOK + t + 1)
                    last = pe.transpose(tp[:, n // 2, (n % 2) * S + t * P:(n % 2) * S + (t + 1) * P],
                                        proj[:, t, n * P:(n + 1) * P], ident[:])
                    if t == TOK - 1:
                        last.then_inc(proj_t, 1)

            def project(v, tiles, kts, act_tiles, m0):
                w = ring_index(v) % RING
                pe.wait_ge(lo_done, v + 1)
                for n in range(tiles):
                    m = m0 + n
                    if m >= 4:
                        pe.wait_ge(comb_done, m - 3)
                    for k in range(kts):
                        last = pair(m % 4, w, (n * kts + k) * P, act_tiles[:, k, :, :], k == 0, k == kts - 1)
                    last.then_inc(acc_full, 1)

            pe.wait_ge(proj_done, 3 * TOK)
            pe.wait_ge(c_lo, KQ)
            for half in range(4):
                project(2 * R_QIDX + half, 2, KQ, cq_t, M_QIDX + 2 * half)

            pe.wait_ge(c_hi, KQ + KV + 1)
            pe.wait_ge(c_lo, KQ + KV)
            for h in range(IDX_HEADS):
                pe.wait_ge(comb_done, h // 2 + 1)
                if h >= 4:
                    pe.wait_ge(relu_done, h - 3)
                rows = slice(IDX_DIM * (h % 2), IDX_DIM * (h % 2) + IDX_DIM)
                for t, c0, n in ((0, 0, P), (1, P, S)):
                    last = pe.matmul(tp[:, h % 4, c0:c0 + n], qidx_t[rows, h // 2, t * P:(t + 1) * P],
                                     kidx_t[rows, 0:n], start=True, stop=True)
                last.then_inc(logits_full, 1)

            def piece(s):
                g, j = divmod(s, 4)
                m0 = M_GROUP + g * M_PER_GROUP
                v = 2 * R_GROUP + s
                if j < 2:
                    project(v, 2, KQ, cq_t, m0 + 2 * j)
                elif j == 2:
                    project(v, GH, KV, ckv_t, m0 + GH)
                else:
                    w = ring_index(v) % RING
                    pe.wait_ge(lo_done, v + 1)
                    for t in range(TOK):
                        m = m0 + 2 * GH + t
                        pe.wait_ge(comb_done, m - 3)
                        steps = [(k, x, wp) for k in range(KV) for x, wp in ((0, w_hi), (0, w_lo), (1, w_hi))]
                        for n, (k, x, wp) in enumerate(steps):
                            last = pe.matmul(acc[:, m % 4, :], ckv_t[:, k, x, t * P:(t + 1) * P],
                                             wp[:, w, k * 512:(k + 1) * 512], start=(n == 0),
                                             stop=(n == len(steps) - 1))
                        last.then_inc(acc_full, 1)

            for s in range(4):
                piece(s)
            pe.wait_ge(relu_done, IDX_HEADS)

            def wide(bank0, lhs, w, k_n, stop):
                def product(t, k, n):
                    for x, part in ((0, w_hi), (0, w_lo), (1, w_hi)):
                        last = pe.matmul(acc[:, bank0 + t, :], lhs[:, k, x, t * P:(t + 1) * P],
                                         part[:, w, n * GC:(n + 1) * GC],
                                         start=(k == 0 and x == 0 and part is w_hi),
                                         stop=(stop and (k, n) == k_n[-1] and x == 1))
                    return last

                if stop:
                    for k, n in k_n:
                        last = product(0, k, n)
                    last.then_inc(acc_t0_full, 1)
                    for k, n in k_n:
                        last = product(1, k, n)
                    last.then_inc(acc_full, 1)
                    return None
                for k, n in k_n:
                    for t in range(TOK):
                        last = product(t, k, n)
                return last

            def out_k(ks, g):
                h = ks[0] // OUT_K
                if ks[0] == 0 and g <= 1:
                    pe.wait_ge(comb_done, M_OUT - 2 + 2 * g)
                elif ks[0] == 0:
                    pe.wait_ge(res_done, TOK * (g - 1))
                if ks[0] % OUT_K == 0:
                    pe.wait_ge(lo_done, 2 * R_OUT + OUT_HALVES * g + h + 1)
                if g == 0:
                    pe.wait_ge(o_lo, ks[-1] + 1)
                end = ks[-1] == KD - 1
                last = wide(2 * (g % 2), o_t, h % RING, [(k, k % OUT_K) for k in ks], end)
                if ks[-1] % OUT_K == OUT_K - 1 and not end:
                    last.then_inc(pe_used, 1)

            out_parts = {12: (0,), 13: (1,), 14: (2,), 15: (3,), 16: (4,), 17: (5, 6), 18: (7,)}
            for s in range(HEADS + 3):
                if s < HEADS:
                    g, h = divmod(s, GH)
                    pe.wait_ge(comb_done, M_GROUP + g * M_PER_GROUP + 2 * GH)
                    if s >= 2:
                        pe.wait_ge(neg_done, s - 1)
                    for t, c0, n in ((0, 0, P), (1, P, S)):
                        last = pe.matmul(tp[:, s % 2, c0:c0 + n], q_t[:, g % 2, h, t * P:(t + 1) * P],
                                         k_t[:, g % 2, h, 0:n], start=True, stop=True)
                    last.then_inc(qk_full, 1)
                if s + 4 < HEADS:
                    piece(s + 4)
                for k in out_parts.get(s, ()):
                    out_k((k,), 0)
                if 2 <= s < HEADS + 2:
                    u = s - 2
                    pe.wait_ge(prob_done, 2 * u + 2)
                    if u >= 1:
                        pe.wait_ge(pt_done, u)
                    for n in range(KEYS // P):
                        last = pe.transpose(tp[:, 2, n * P:(n + 1) * P], prob[:, u % 3, n * P:(n + 1) * P],
                                            ident[:])
                    last.then_inc(pt_full, 1)
                if s >= 3:
                    u = s - 3
                    g, h = divmod(u, GH)
                    pe.wait_ge(pt_done, u + 1)
                    if u >= 1:
                        pe.wait_ge(o_lo, u)
                    pe.wait_ge(comb_done, M_GROUP + (g + 1) * M_PER_GROUP)
                    v_h = [v_n[:, g % 2, t, h * HD:(h + 1) * HD] for t in range(TOK)]
                    pe.matmul(tp[:, 3, 0:P], v_h[0], prob_t[:, u % 2, 0:P], start=True, stop=True)
                    pe.matmul(tp[:, 3, P:S], v_h[0], prob_t[:, u % 2, P:2 * P], start=True, stop=False)
                    pe.matmul(tp[:, 3, P:S], v_h[1], prob_t[:, u % 2, 2 * P:3 * P], start=False,
                              stop=True).then_inc(pv_full, 1)

            for g in range(COL_GROUPS):
                for k in range(8 if g == 0 else 0, KD, OUT_K):
                    out_k(range(k, k + OUT_K), g)

            def turn_in(k):
                if k % 4 == 0:
                    c = k // 4
                    pe.wait_ge(xhat_done, c + 1 + max(0, c + 1 - ACT_XHAT))
                    pe.wait_ge(xhat_act, min(c + 1, ACT_XHAT))
                if k % 2 == 0 and k >= 8:
                    pe.wait_ge(xt_hi, k - 6)
                    pe.wait_ge(xt_val, k - 6)
                for t in range(TOK):
                    c0 = (k % 2) * S + t * P
                    last = pe.transpose(tp[:, (k // 2) % 4, c0:c0 + P], xn[:, t, k * P:(k + 1) * P], ident[:])
                last.then_inc(xt_full, 1)

            for k in range(8):
                turn_in(k)

            def first_tile():
                for n in range(2):
                    for j in (2 * n, 2 * n + 1):
                        pe.wait_ge(lo_done, 2 * R_FFN + j + 1)
                    for k in range(8 * n, 8 * n + 8):
                        pe.wait_ge(xt_lo, len([u for u in range(k + 1) if u not in POOL_LO]))
                        if k in POOL_LO:
                            pe.wait_ge(xt_lo_pool, len([u for u in POOL_LO if u <= k]))
                        for j in (2 * n, 2 * n + 1):
                            last = pair(j % 2, j, (k % 8) * P, act_t[:, k, :, :], k == 0, k == KD - 1)
                            if k % 8 == 7:
                                last.then_inc(*((pe_used, 1) if j < 3 else (ffn_full, 1)))
                        if k % 2 == 1 and k < 8:
                            turn_in(k + 7)
                            turn_in(k + 8)

            def ffn_tile(c, i):
                tile = 2 * i + c
                if not (isinstance(i, int) and i == 0):
                    pe.wait_ge(ffn_comb, tile - 1)
                for j in range(4):
                    pe.wait_ge(lo_done, 2 * R_FFN + 4 * tile + j + 1)
                    for n in range(8):
                        k = 8 * (j % 2) + n
                        last = pair(2 * c + j // 2, j, n * P, act_t[:, k, :, :], k == 0, k == KD - 1)
                    last.then_inc(*((pe_used, 1) if j < 3 else (ffn_full, 1)))

            first_tile()
            ffn_tile(1, 0)
            with pe.Fori(1, KF // 2) as i:
                ffn_tile(0, i)
                ffn_tile(1, i)

            def down_group(c, i):
                g = 2 * i + c
                pe.wait_ge(res_done, TOK * (COL_GROUPS - 1 + g))
                pe.wait_ge(ffn_comb, KF - 1 + c)
                for h in range(len(DOWN_K)):
                    pe.wait_ge(lo_done, 2 * R_DOWN + len(DOWN_K) * g + h + 1)
                    if c == 0 and h in (0, len(DOWN_K) - 1):
                        pe.wait_ge(ffn_lo, KF - 2 if h == 0 else KF)
                    end = h == len(DOWN_K) - 1
                    last = wide(2 * c, hid_t, h % RING, [(DOWN_K0[h] + n, n) for n in range(DOWN_K[h])],
                                end)
                    if not end:
                        last.then_inc(pe_used, 1)

            with pe.Fori(0, COL_GROUPS // 2) as i:
                down_group(0, i)
                down_group(1, i)


_OUT = ((1, S, D), "float32")


def kernel(**inputs):
    from concourse import bacc
    from concourse.bass_utils import run_bass_kernel_spmd

    w = {n: np.asarray(v) for n, v in inputs.items()}

    def k_tiles(m, cols):
        k, n = m.shape
        return m.reshape(k // P, P, n // cols, cols).transpose(2, 1, 0, 3).reshape(n // cols, P, -1)

    x = w["x"].reshape(S, D)
    uq = k_tiles(w["l0_w_uq"], P).reshape(GROUPS, GH, P, -1).transpose(0, 2, 1, 3).reshape(GROUPS, P, -1)
    uk = w["l0_w_uk"].reshape(GROUPS, GH, HD, KV, P).transpose(0, 4, 1, 3, 2).reshape(GROUPS, P, -1)
    uv = w["l0_w_uv"].reshape(GROUPS, GH, KV, P, HD).transpose(0, 3, 2, 1, 4).reshape(GROUPS, P, -1)
    gate, up = (k_tiles(w[n], P) for n in ("l0_ffn_gate", "l0_ffn_up"))
    arrays = {
        "x": x,
        "x_t": x.T.reshape(2, 8, P, S).transpose(0, 2, 1, 3).reshape(2, P, -1),
        "w_in": w["l0_w_in"].reshape(8, 2, P, W_IN).transpose(0, 2, 1, 3).reshape(8, P, -1),
        "w_qidx": k_tiles(w["l0_w_qidx"], P).reshape(2, 4, P, -1).transpose(0, 2, 1, 3).reshape(2, P, -1),
        "w_uq": uq,
        "w_ukv": np.concatenate([uk, uv], axis=2),
        "w_out": k_tiles(w["l0_w_out"], GC),
        "w_gu": np.stack([gate, up], axis=1).reshape(2 * KF, P, -1),
        "w_down": k_tiles(w["l0_ffn_down"], GC),
        "rms_g_t": np.concatenate([w["l0_q_norm"].reshape(KQ, P), w["l0_kv_norm"].reshape(KV, P)]).T,
        "ln1_gb_t": np.stack([w["l0_ln1_g"], w["l0_ln1_b"]]).reshape(2, KD, P).transpose(2, 0, 1),
        "ln_rows": np.stack([w["l0_ln1_g"], w["l0_ln1_b"], w["l0_ln2_g"], w["l0_ln2_b"]]),
    }
    nc = bacc.Bacc("TRN2", target_bir_lowering=False, num_devices=1)
    feed, aps = {}, {}
    for name, value in arrays.items():
        value = np.ascontiguousarray(value)
        feed["in_" + name] = value
        aps[name] = nc.dram_tensor("in_" + name, value.shape, mybir.dt.from_np(value.dtype),
                                   kind="ExternalInput").ap()
    aps["out"] = nc.dram_tensor("out_0", (S, D), F32, kind="ExternalOutput").ap()
    layer_kernel(nc, aps)
    r = run_bass_kernel_spmd(nc, [feed], core_ids=[0])
    return r.results[0]["out_0"].reshape(_OUT[0])
```
